# Optimizing a Trainium2 kernel written in Bass

```python
import jax, jax.numpy as jnp
from jax import lax
import numpy as np

D_MODEL = 2048
BATCH = 1
SEQ = 512
DEPTH = 1

CTX_LEN = 256
GRID_W = 64
MIX_WIDTH = D_MODEL
A_WIDTH = MIX_WIDTH // 2
A_HEADS = 8
A_HEAD_DIM = A_WIDTH // A_HEADS
A_CHUNK = 128
B_WIDTH = MIX_WIDTH - A_WIDTH
B_HEADS = 8
B_HEAD_DIM = B_WIDTH // B_HEADS
HALF_B = B_HEADS // 2
B_CHUNK = 64
D_FF = 4 * D_MODEL
IN_COLS = 2 * A_WIDTH + 5 * B_WIDTH
EPS = 1e-6

kernel_name = "hybrid_gmlp_hgrn2_dit_layer"

def rms_norm(x, gain):
    xf = x.astype(jnp.float32)
    y = xf * lax.rsqrt(jnp.mean(xf * xf, axis=-1, keepdims=True) + EPS)
    return (y * gain.astype(jnp.float32)).astype(x.dtype)

def modulate(h, shift, scale):
    return h * (1 + scale[:, None, :]) + shift[:, None, :]

def adaln(cond, w, b):
    return jnp.split(jax.nn.silu(cond) @ w + b, 6, axis=-1)

def to_col_major(a, rows):
    return a.reshape(a.shape[0], rows, GRID_W, *a.shape[2:]).swapaxes(1, 2).reshape(a.shape)

def from_col_major(a, rows):
    return a.reshape(a.shape[0], GRID_W, rows, *a.shape[2:]).swapaxes(1, 2).reshape(a.shape)

def scan_order(a, rows):
    return jnp.concatenate([a[:, :, :HALF_B], to_col_major(a[:, :, HALF_B:], rows)], axis=2)

def raster_order(a, rows):
    return jnp.concatenate([a[:, :, :HALF_B], from_col_major(a[:, :, HALF_B:], rows)], axis=2)

def gmlp_group(u, v, w_s, b_s, v_gain):
    n, t, _ = u.shape
    u = jax.nn.gelu(u).reshape(n, t, A_HEADS, A_HEAD_DIM)
    v = rms_norm(jax.nn.gelu(v).reshape(n, t, A_HEADS, A_HEAD_DIM), v_gain)
    vc = v.reshape(n, t // A_CHUNK, A_CHUNK, A_HEADS, A_HEAD_DIM)
    mixed = jnp.einsum('hts,bnshd->bnthd', w_s, vc) + b_s.T[None, None, :, :, None]
    return (u * mixed.reshape(u.shape)).reshape(n, t, A_WIDTH)

def hgrn2_chunk_scan(q, k, v, log_f):
    n, h, t, dk = q.shape
    dv = v.shape[-1]
    nc = t // B_CHUNK

    def to_chunks(a):
        return jnp.moveaxis(a.reshape(n, h, nc, B_CHUNK, a.shape[-1]), 2, 0)

    within_dir = jnp.tril(jnp.ones((B_CHUNK, B_CHUNK), bool))

    def step(state, inp):
        qi, ki, vi, gi = inp
        b = jnp.cumsum(gi, axis=2)
        o_inter = jnp.einsum('nhtk,nhkv->nhtv', qi * jnp.exp(b), state)
        diff = jnp.where(within_dir[None, None, :, :, None],
                         b[:, :, :, None, :] - b[:, :, None, :, :], -jnp.inf)
        scores = jnp.einsum('nhtk,nhsk,nhtsk->nhts', qi, ki, jnp.exp(diff))
        o_intra = jnp.einsum('nhts,nhsv->nhtv', scores, vi)
        b_last = b[:, :, -1:, :]
        new_state = (jnp.exp(b_last[:, :, 0, :])[..., None] * state
                     + jnp.einsum('nhsk,nhsv->nhkv', ki * jnp.exp(b_last - b), vi))
        return new_state, o_inter + o_intra

    s0 = jnp.zeros((n, h, dk, dv), jnp.float32)
    _, out = lax.scan(step, s0, tuple(map(to_chunks, (q, k, v, log_f))))
    return jnp.moveaxis(out, 0, 2).reshape(n, h, t, dv)

def hgrn2_group(lat, cx, lb, o_gain, rows, with_ctx):
    def heads(a):
        return a.reshape(a.shape[0], a.shape[1], B_HEADS, B_HEAD_DIM).astype(jnp.float32)

    flip = lambda a: jnp.flip(a, axis=1)
    q_l, i_l, ff_l, fb_l = (scan_order(heads(a), rows) for a in lat[:4])
    q_c, i_c, ff_c, fb_c = (heads(a) for a in cx[:4])
    n_ctx = q_c.shape[1]
    bsz = q_l.shape[0]
    fwd = [jnp.concatenate([a, b], axis=1) for a, b in ((q_c, q_l), (i_c, i_l), (ff_c, ff_l))]
    bwd = [jnp.concatenate([flip(a), flip(b)], axis=1) for a, b in ((q_c, q_l), (i_c, i_l), (fb_c, fb_l))]
    q, v, z = (jnp.stack([f_, b_]) for f_, b_ in zip(fwd, bwd))
    t = q.shape[2]
    lbd = lb.astype(jnp.float32).reshape(2, 1, 1, B_HEADS, B_HEAD_DIM)
    f = lbd + (1 - lbd) * jax.nn.sigmoid(z)
    k = 1 - f

    def to_scan(a):
        return jnp.moveaxis(a.reshape(2 * bsz, t, B_HEADS, a.shape[-1]), 1, 2)

    out = hgrn2_chunk_scan(to_scan(q), to_scan(k), to_scan(v), to_scan(jnp.log(f)))
    out = jnp.moveaxis(out, 2, 1).reshape(2, bsz, t, B_HEADS, B_HEAD_DIM)
    o_fwd, o_bwd = out[0], out[1]

    def readout(o, g):
        y = rms_norm(o, o_gain) * jax.nn.silu(heads(g))
        return y.reshape(y.shape[0], y.shape[1], B_WIDTH).astype(g.dtype)

    o_lat = raster_order(o_fwd[:, n_ctx:] + flip(o_bwd[:, n_ctx:]), rows)
    y_lat = readout(o_lat, lat[4])
    y_ctx = readout(o_fwd[:, :n_ctx] + flip(o_bwd[:, :n_ctx]), cx[4]) if with_ctx else None
    return y_lat, y_ctx

def token_mixer(h_lat, h_ctx, w_in, w_s, b_s, v_gain, lb, o_gain, rows, with_ctx):
    cuts = [A_WIDTH, 2 * A_WIDTH, 2 * A_WIDTH + B_WIDTH, 2 * A_WIDTH + 2 * B_WIDTH,
            2 * A_WIDTH + 3 * B_WIDTH, 2 * A_WIDTH + 4 * B_WIDTH]
    lat = jnp.split(h_lat @ w_in, cuts, axis=-1)
    cx = jnp.split(h_ctx @ w_in, cuts, axis=-1)
    a_lat = gmlp_group(lat[0], lat[1], w_s, b_s, v_gain)
    b_lat, b_ctx = hgrn2_group(lat[2:], cx[2:], lb, o_gain, rows, with_ctx)
    mix_lat = jnp.concatenate([a_lat, b_lat], axis=-1)
    if not with_ctx:
        return mix_lat, None
    a_ctx = gmlp_group(cx[0], cx[1], w_s, b_s, v_gain)
    return mix_lat, jnp.concatenate([a_ctx, b_ctx], axis=-1)

def squared_relu_mlp(h, w1, w2):
    return jnp.square(jax.nn.relu(h @ w1)) @ w2

def setup_inputs(seed: int = 0) -> dict:
    key = jax.random.key(seed)
    ks = jax.random.split(key, 19)
    nrm = jax.random.normal
    d = D_MODEL
    return {
        "x": nrm(ks[0], (BATCH, SEQ, d), jnp.float32),
        "c": nrm(ks[1], (BATCH, d), jnp.float32),
        "ctx": nrm(ks[2], (BATCH, CTX_LEN, d), jnp.float32),
        "c_ctx": nrm(ks[3], (d,), jnp.float32),
        "w_ada": nrm(ks[4], (DEPTH, d, 6 * d), jnp.float32) * d ** -0.5,
        "b_ada": 0.02 * nrm(ks[5], (DEPTH, 6 * d), jnp.float32),
        "norm1_gain": 1.0 + 0.05 * nrm(ks[6], (DEPTH, d), jnp.float32),
        "w_in": nrm(ks[7], (DEPTH, d, IN_COLS), jnp.float32) * d ** -0.5,
        "gmlp_w_s": nrm(ks[8], (DEPTH, A_HEADS, A_CHUNK, A_CHUNK), jnp.float32) * A_CHUNK ** -0.5,
        "gmlp_b_s": 1.0 + 0.05 * nrm(ks[9], (DEPTH, A_HEADS, A_CHUNK), jnp.float32),
        "gmlp_v_gain": 1.0 + 0.05 * nrm(ks[10], (DEPTH, A_HEADS, A_HEAD_DIM), jnp.float32),
        "hgrn_lb_logits": 0.1 * nrm(ks[11], (DEPTH + 1, 2, B_WIDTH), jnp.float32),
        "hgrn_o_gain": 1.0 + 0.05 * nrm(ks[12], (DEPTH, B_HEADS, B_HEAD_DIM), jnp.float32),
        "w_out": nrm(ks[13], (DEPTH, MIX_WIDTH, d), jnp.float32) * MIX_WIDTH ** -0.5,
        "norm2_gain": 1.0 + 0.05 * nrm(ks[14], (DEPTH, d), jnp.float32),
        "w_ff1": nrm(ks[15], (DEPTH, d, D_FF), jnp.float32) * d ** -0.5,
        "w_ff2": nrm(ks[16], (DEPTH, D_FF, d), jnp.float32) * D_FF ** -0.5,
        "final_gain": 1.0 + 0.05 * nrm(ks[17], (d,), jnp.float32),
    }

def reference(x, c, ctx, c_ctx, w_ada, b_ada, norm1_gain, w_in, gmlp_w_s, gmlp_b_s, gmlp_v_gain,
              hgrn_lb_logits, hgrn_o_gain, w_out, norm2_gain, w_ff1, w_ff2, final_gain):
    rows = x.shape[1] // GRID_W
    cum = jnp.cumsum(jax.nn.softmax(hgrn_lb_logits.astype(jnp.float32), axis=0), axis=0)
    lb_all = cum[1:] - cum[:1]
    for layer in range(DEPTH):
        with_ctx = layer < DEPTH - 1
        sh1, sc1, g1, sh2, sc2, g2 = adaln(c, w_ada[layer], b_ada[layer])
        csh1, csc1, cg1, csh2, csc2, cg2 = adaln(c_ctx[None, :], w_ada[layer], b_ada[layer])
        h_lat = modulate(rms_norm(x, norm1_gain[layer]), sh1, sc1)
        h_ctx = modulate(rms_norm(ctx, norm1_gain[layer]), csh1, csc1)
        mix_lat, mix_ctx = token_mixer(h_lat, h_ctx, w_in[layer], gmlp_w_s[layer], gmlp_b_s[layer],
                                       gmlp_v_gain[layer], lb_all[layer], hgrn_o_gain[layer],
                                       rows, with_ctx)
        x = x + g1[:, None, :] * (mix_lat @ w_out[layer])
        h = modulate(rms_norm(x, norm2_gain[layer]), sh2, sc2)
        x = x + g2[:, None, :] * squared_relu_mlp(h, w_ff1[layer], w_ff2[layer])
        if with_ctx:
            ctx = ctx + cg1[:, None, :] * (mix_ctx @ w_out[layer])
            hc = modulate(rms_norm(ctx, norm2_gain[layer]), csh2, csc2)
            ctx = ctx + cg2[:, None, :] * squared_relu_mlp(hc, w_ff1[layer], w_ff2[layer])
    return rms_norm(x, final_gain)


_drawn_inputs = setup_inputs


def setup_inputs(seed=0):
    import zlib

    import numpy as np

    out = dict(_drawn_inputs(seed))
    spreads = {}
    factors = {'ctx': 4.505,
     'c_ctx': 4.182,
     'gmlp_b_s': 3.442,
     'gmlp_v_gain': 3.547,
     'hgrn_lb_logits': 3.096,
     'hgrn_o_gain': 4.019}
    for name, (base, spread) in spreads.items():
        noise = np.random.default_rng([zlib.crc32(name.encode()), seed]).standard_normal(out[name].shape)
        drawn = base * np.exp(spread * noise) if base else spread * noise
        out[name] = __import__('jax').numpy.asarray(drawn.astype(out[name].dtype))
    for name, factor in factors.items():
        out[name] = (out[name] * factor).astype(out[name].dtype)
    return out
```

```python
from contextlib import ExitStack

import concourse.bass as bass
from concourse import mybir

F32 = mybir.dt.float32
F32R = mybir.dt.float32r
U8 = mybir.dt.uint8
ACT = mybir.ActivationFunctionType
ALU = mybir.AluOpType
AX = mybir.AxisListType

P = 128
D = 2048
KT = D // P
SEQ, CTX = 512, 256
TT, CT = SEQ // P, CTX // P
HEADS = 8
ROWS, GRID_W = 8, 64
DFF = 8192
BLOCKS = 8
HT = DFF // BLOCKS // P
UNIT = 1024
LEVELS = 7
EPS = 1e-6
KB = 1024

U_CTX_V = 0
U_CTX_HEADS = U_CTX_V + 16
U_V = U_CTX_HEADS + 4 * HEADS
U_HEADS = U_V + 16
U_GU = U_HEADS + 8 * HEADS
U_GV = U_GU + 16
U_OUT = U_GV + 16
U_MLP = U_OUT + 32
UNITS = U_MLP + 32 * BLOCKS

ADA_CHUNKS = 16

STEP_SLOTS = {0: [0, 1], 1: [2], 3: [3], 4: [4], 5: [5], 7: [6], 8: [7], 9: [8], 11: [9], 12: [10], 15: [11]}


def build(nc, ctx_x, x, w_stream, w_ada, cols, small, masks, bs_row, final_row, ws_t, out):
    with ExitStack() as stack:
        base = nc.sbuf_base
        top = nc.sbuf_usable_end
        where = [base + (-base) % 32]

        def fixed(name, shape, dt=F32):
            n = 1 if dt == U8 else 4
            for s in shape[1:]:
                n *= s
            t = nc.alloc_sbuf_tensor_at(name, shape, dt, offset=where[0])
            where[0] += n + (-n) % 32
            return t

        raw = fixed("raw", [P, 4, UNIT])
        w_hi = fixed("w_hi", [P, 2, UNIT], F32R)
        w_lo = fixed("w_lo", [P, 2, UNIT], F32R)
        r1 = where[0]
        h_hi = fixed("h_hi", [P, KT, SEQ], F32R)
        h_lo = fixed("h_lo", [P, KT, SEQ], F32R)
        ada1_w = nc.alloc_sbuf_tensor_at("ada1_w", [P, 4, 4096], F32, offset=r1)
        junk = nc.alloc_sbuf_tensor_at("junk", [P, D], F32, offset=r1)
        ident = fixed("ident", [P, P])
        ones = fixed("ones", [P, 8])
        mask = fixed("mask", [P, LEVELS, P], U8)
        col = fixed("col", [P, 192])
        cs = fixed("cs", [P, KT, 2])
        mod1 = fixed("mod1", [P, 2, KT, 2])
        mod2 = fixed("mod2", [P, 4, KT])
        lb = fixed("lb", [P, 2, HEADS])
        oml = fixed("oml", [P, 2, HEADS])
        lbt = fixed("lbt", [P, 3, 2 * HEADS])
        stat = fixed("stat", [P, 64])
        w0 = where[0]
        assert w0 + 108 * KB <= top, (w0, top)

        def work(name, kb, shape, dt=F32):
            return nc.alloc_sbuf_tensor_at(name, shape, dt, offset=w0 + int(kb * KB))

        C_COL = col[:, 0:32].rearrange("p (k c) -> p k c", c=2)
        B1_COL = col[:, 32:64]
        B2_COL = col[:, 64:128]
        N1_COL, N2_COL = col[:, 128:144], col[:, 144:160]
        VG_COL, OG_COL = col[:, 160:168], col[:, 168:176]
        lbl = fixed("lbl", [P, 2, 2 * HEADS])
        w0 = where[0]
        assert w0 + 108 * KB <= top, (w0, top)

        c_hi = work("c_hi", 0, [P, KT, CTX], F32R)
        c_lo = work("c_lo", 16, [P, KT, CTX], F32R)
        ctx_tok = work("ctx_tok", 32, [P, CT, D])
        v_ctx = work("v_ctx", 48, [P, CT, 1024])
        x_tok = work("x_tok", 56, [P, TT, D])
        prep_tmp = work("prep_tmp", 88, [P, 2, SEQ])
        c_sig = work("c_sig", 88, [P, 2, CTX])
        c_f = work("c_f", 90, [P, 2, CTX])
        c_k = work("c_k", 92, [P, 2, CTX])
        c_decay = work("c_decay", 94, [P, 2, CTX])
        c_kd = work("c_kd", 96, [P, 2, CTX])
        c_ktok = work("c_ktok", 98, [P, 4, P])
        mask_f32 = work("mask_f32", 100, [P, LEVELS, P])
        s_ctx = work("s_ctx", 100, [P, HEADS, 2, P])
        v_lat = work("v_lat", 0, [P, TT, 1024])
        v_cols = work("v_cols", 16, [P, 2, SEQ])
        mix = work("mix", 16, [P, KT, SEQ])
        q_sb = work("q_sb", 48, [P, SEQ])
        sig = work("sig", 50, [P, 2, SEQ])
        g_sb = work("g_sb", 54, [P, SEQ])
        tot = work("tot", 56, [P, 2, 1024])
        xx = work("xx", 64, [P, 2, SEQ])
        yy = work("yy", 68, [P, 2, SEQ])
        ksum = work("ksum", 72, [P, SEQ])
        score = work("score", 74, [P, TT, P])
        ktok = work("ktok", 76, [P, 6, P])
        state = work("state", 79, [P, 2, 3, P])
        o_norm = work("o_norm", 82, [P, TT, P])
        ada_w = work("ada_w", 85, [P, 2, 2, 512])
        ada_acc = work("ada_acc", 93, [P, 512])
        o_sq = work("o_sq", 95, [P, TT, P])
        gv = work("gv", 0, [P, 2, TT, 512])
        g1_row = work("g1_row", 48, [P, D])
        g2_row = work("g2_row", 56, [P, D])
        g_tmp = work("g_tmp", 64, [P, 2, 512])
        x_res = work("x_res", 68, [P, TT, D])
        ws = work("ws", 100, [P, HEADS, P])
        bs = work("bs", 104, [P, HEADS, P])
        relu_sb = work("relu_sb", 0, [P, 2, SEQ])
        hid_sb = work("hid_sb", 4, [P, 2, SEQ])
        fin_row = work("fin_row", 8, [P, D])
        x_norm = work("x_norm", 16, [P, TT, D])
        hid_hi = work("hid_hi", 16, [P, HT, SEQ], F32R)
        hid_lo = work("hid_lo", 32, [P, HT, SEQ], F32R)
        prep_tmp2 = work("prep_tmp2", 0, [P, 2, SEQ])

        bank = [stack.enter_context(nc.psum_tensor(f"bank{i}", [P, 512], F32)) for i in range(8)]

        def sem(name):
            return stack.enter_context(nc.semaphore(name))

        raw_landed = [sem(f"raw_landed{i}") for i in range(4)]
        hi_done, lo_done, unit_used = sem("hi_done"), sem("lo_done"), sem("unit_used")
        small_landed, ctx_landed, x_landed = sem("small_landed"), sem("ctx_landed"), sem("x_landed")
        ada1_landed = [sem(f"ada1_landed{i}") for i in range(4)]
        ada1_used, ada1_done = sem("ada1_used"), sem("ada1_done")
        cs_ready, ones_ready, mod1_ready, mod1_step = sem("cs_ready"), sem("ones_ready"), sem("mod1_ready"), sem("mod1_step")
        lb_step, lb_exp, lb_ready = sem("lb_step"), sem("lb_exp"), sem("lb_ready")
        mask_ready = sem("mask_ready")
        sumsq, root, rstd, normed = sem("sumsq"), sem("root"), sem("rstd"), sem("normed")
        turned, prep_hi, prep_h, prep_lo = sem("turned"), sem("prep_hi"), sem("prep_h"), sem("prep_lo")
        cv_read = sem("cv_read")
        c_scan = sem("c_scan")
        cgate_read, c_step, c_kd_ready = sem("cgate_read"), sem("c_step"), sem("c_kd_ready")
        c_turned, c_ktok_ready, c_state_done, s_ctx_ready = sem("c_turned"), sem("c_ktok_ready"), sem("c_state_done"), sem("s_ctx_ready")
        vt_made, v_turned = sem("vt_made"), sem("v_turned")
        v_read, proj_read = sem("v_read"), sem("proj_read")
        gate_step, scan_ready = sem("gate_step"), sem("scan_ready")
        scores_done, scores_merged, level_ready, tot_ready = sem("scores_done"), sem("scores_merged"), sem("level_ready"), sem("tot_ready")
        k_turned, ktok_ready, kv_done, states_ready = sem("k_turned"), sem("ktok_ready"), sem("kv_done"), sem("states_ready")
        o_done, o_root, o_rstd, o_ready, o_turned, head_out = sem("o_done"), sem("o_root"), sem("o_rstd"), sem("o_ready"), sem("o_turned"), sem("head_out")
        ada_landed = [sem(f"ada_landed{i}") for i in range(2)]
        ada_summed, ada_colsum, mod2_made, mod2_step = sem("ada_summed"), sem("ada_colsum"), sem("mod2_made"), sem("mod2_step")
        row_done, row_read = sem("row_done"), sem("row_read")
        u_read, gv_read = sem("u_read"), sem("gv_read")
        gv_step, gv_root, gv_ready, ws_landed = sem("gv_step"), sem("gv_root"), sem("gv_ready"), sem("ws_landed")
        gv_rstd, mixed_head = sem("gv_rstd"), sem("mixed_head")
        mixed_step, mix_a_ready = sem("mixed_step"), sem("mix_a_ready")
        split_hi, split_lo, x_res_landed = sem("split_hi"), sem("split_lo"), sem("x_res_landed")
        out_done, out_tmp, x_res_ready = sem("out_done"), sem("out_tmp"), sem("x_res_ready")
        relu_made, hid_made, hid_hi_made, hid_ready = sem("relu_made"), sem("hid_made"), sem("hid_hi_made"), sem("hid_ready")
        ff2_done, ff2_tmp, ff2_added = sem("ff2_done"), sem("ff2_tmp"), sem("ff2_added")
        fin_landed, fin_ready, stored = sem("fin_landed"), sem("fin_ready"), sem("stored")

        block = stack.enter_context(nc.Block())

        @block.sync
        def _(sp):
            for t in range(CT):
                sp.dma_start(ctx_tok[:, t], ctx_x[t * P:(t + 1) * P, :]).then_inc(ctx_landed, 16)

            def load_ada1(i, s, first):
                if not first:
                    sp.wait_ge(ada1_used, 4 * (i - 1) + s + 1)
                sp.dma_start(ada1_w[:, s], w_ada[bass.ds((4 * i + s) * P, P), 0:4096]).then_inc(ada1_landed[s], 16)

            for s in range(4):
                load_ada1(0, s, True)
            with sp.Fori(1, KT // 4) as i:
                for s in range(4):
                    load_ada1(i, s, False)

            def load_unit(q, r, first=False):
                if not first:
                    sp.wait_ge(lo_done, 4 * (q - 1) + r + 1)
                sp.dma_start(raw[:, r], w_stream[bass.ds(4 * q + r, 1)].rearrange("a p n -> (a p) n")).then_inc(raw_landed[r], 16)

            def load_ada2(n, m):
                if not (isinstance(n, int) and n == 0 and m < 2):
                    sp.wait_ge(ada_summed, 16 * n + 2 * m - 2)
                src = w_ada[2 * m * P:(2 * m + 2) * P, bass.ds(4096 + 512 * n, 512)]
                sp.dma_start(ada_w[:, m % 2], src.rearrange("(t p) c -> p t c", p=P)).then_inc(ada_landed[m % 2], 16)

            for r in range(4):
                load_unit(0, r, True)
            sp.wait_ge(sumsq, CT)
            for t in range(TT):
                sp.dma_start(x_tok[:, t], x[t * P:(t + 1) * P, :]).then_inc(x_landed, 16)
            with sp.Fori(1, U_V // 4) as q:
                for r in range(4):
                    load_unit(q, r)

            def load_both(q, n):
                for r in range(4):
                    load_unit(q, r)
                    load_ada2(n, 2 * r)
                    load_ada2(n, 2 * r + 1)

            for r in range(4):
                load_unit(U_V // 4, r)
            sp.wait_ge(c_kd_ready, 2 * HEADS)
            for m in range(8):
                load_ada2(0, m)
            with sp.Fori(1, 4) as n:
                load_both(n + U_V // 4, n)
            with sp.Fori(0, HEADS) as h:
                for r in range(8):
                    load_unit(2 * h + (U_HEADS // 4 + r // 4), r % 4)
                    load_ada2(h + 4, r)
            for r in range(8):
                load_unit(U_GU // 4 + r // 4, r % 4)
                load_ada2(12, r)
            with sp.Fori(13, 16) as n:
                load_both(n + (U_GU // 4 - 11), n)
            sp.dma_start(ws[:], ws_t).then_inc(ws_landed, 16)
            sp.dma_start(bs[:], bs_row.partition_broadcast(P)).then_inc(ws_landed, 16)
            for r in range(4):
                load_unit(U_GV // 4 + 1, r)
            sp.wait_ge(mod2_made, 16)
            for t in range(TT):
                sp.dma_start(x_res[:, t], x[t * P:(t + 1) * P, :]).then_inc(x_res_landed, 16)
            with sp.Fori(U_GV // 4 + 2, U_MLP // 4) as q:
                for r in range(4):
                    load_unit(q, r)
            sp.wait_ge(mixed_step, 8)
            sp.dma_start(fin_row[:], final_row.partition_broadcast(P)).then_inc(fin_landed, 16)
            with sp.Fori(U_MLP // 4, UNITS // 4) as q:
                for r in range(4):
                    load_unit(q, r)
            for t in range(TT):
                sp.wait_ge(fin_ready, t + 1)
                sp.dma_start(out[t * P:(t + 1) * P, :], x_res[:, t]).then_inc(stored, 16)
            sp.wait_ge(stored, 16 * TT)

        @block.gpsimd
        def _(pool):
            with pool.Fori(0, UNITS // 4) as q:
                for r in range(4):
                    pool.wait_ge(hi_done, 4 * q + r + 1)
                    pool.tensor_tensor(w_lo[:, r % 2], raw[:, r], w_hi[:, r % 2].bitcast(F32), ALU.subtract).then_inc(lo_done, 1)

        @block.scalar
        def _(act):
            for dst, src in ((col[:], cols), (lbl[:].rearrange("p a b -> p (a b)"), small), (ident[:], masks[0]), ):
                act.dma_start(dst, src).then_inc(small_landed, 16)
            act.dma_start(mask_f32[:], masks[1]).then_inc(small_landed, 16)
            act.wait_ge(small_landed, 64)
            act.activation(cs[:], C_COL, ACT.Silu).then_inc(cs_ready, 1)
            act.wait_ge(lb_step, 2)
            act.activation(lbt[:, 1:3], lbt[:, 1:3], ACT.Exp).then_inc(lb_exp, 1)

            def hi_unit(q, r, static=False):
                if not (static and q == 0 and r < 2):
                    act.wait_ge(unit_used, 4 * q + r - 1)
                act.wait_ge(raw_landed[r], 16 * q + 16)
                act.activation(w_hi[:, r % 2], raw[:, r], ACT.Copy).then_inc(hi_done, 1)

            def hi_next(u0, q, j):
                hi_unit(q + (u0 // 4 + (j + 2) // 4), (j + 2) % 4)

            def roots(n0, count, width, wait_for=True):
                for t in range(count):
                    act.wait_ge(sumsq, n0 + t + 1)
                act.activation(stat[:, n0:n0 + count], stat[:, n0:n0 + count], ACT.Sqrt, bias=stat[:, 63:64], scale=1.0 / width).then_inc(root, 1)

            def prep(n0, count, ntok, hi, s, b):
                for i in range(count):
                    n = n0 + i
                    kt = n % KT
                    act.wait_ge(turned, n + 1)
                    act.activation(hi[:, kt], bank[4 + n % 4][:, 0:ntok], ACT.Identity, bias=b(kt), scale=s(kt)).then_inc(prep_hi, 1)

            act.wait_ge(ones_ready, 2)
            act.wait_ge(ctx_landed, 16 * CT)
            for t in range(CT):
                if t:
                    act.wait_ge(sumsq, t)
                act.activation(x_tok[:, 0], ctx_tok[:, t], ACT.Square, accum_out=stat[:, t:t + 1]).then_inc(sumsq, 1)
            roots(0, CT, D)
            hi_unit(0, 0, True)
            hi_unit(0, 1, True)
            act.wait_ge(mod1_step, 2)
            prep(0, KT, CTX, c_hi, lambda k: mod1[:, 1, k, 1:2], lambda k: mod1[:, 0, k, 1:2])
            for j in range(16):
                hi_next(U_CTX_V, 0, j)
                if j == 0:
                    act.wait_ge(ada1_done, 1)
                if j in (2, 3, 4, 5):
                    t = j - 2
                    act.wait_ge(x_landed, 16 * TT)
                    if t:
                        act.wait_ge(sumsq, CT + t)
                    act.activation(junk[:], x_tok[:, t], ACT.Square, accum_out=stat[:, 2 + t:3 + t]).then_inc(sumsq, 1)
                if j == 5:
                    roots(2, TT, D)
                if j >= 8:
                    prep(KT + 2 * (j - 8), 2, SEQ, h_hi, lambda k: mod1[:, 1, k, 0:1], lambda k: mod1[:, 0, k, 0:1])
                if j % 8 == 7:
                    for t in range(CT):
                        act.wait_ge(unit_used, U_CTX_V + j + 1)
                        act.activation(v_ctx[:, t, (j // 8) * 512:(j // 8 + 1) * 512], bank[2 * (j // 8) + t][:], ACT.Copy).then_inc(cv_read, 1)

            act.wait_ge(prep_lo, 2 * KT)

            def c_ktok_out(h):
                act.wait_ge(c_turned, h + 1)
                act.activation(c_ktok[:], bank[6][:].rearrange("p (a b) -> p a b", b=P), ACT.Copy).then_inc(c_ktok_ready, 1)

            def c_head_act(h, first):
                for j in range(4):
                    hi_next(U_CTX_HEADS, h, j)
                    if j % 2 == 1:
                        d = j // 2
                        act.wait_ge(unit_used, 4 * h + (U_CTX_HEADS + j + 1))
                        if not first:
                            act.wait_ge(c_step, 4 * h)
                        act.activation(c_sig[:, d], bank[d][:, 0:CTX], ACT.Sigmoid).then_inc(cgate_read, 1)
                    if j == 1 and not first:
                        c_ktok_out(h - 1)

            c_head_act(0, True)
            with act.Fori(1, HEADS) as h:
                c_head_act(h, False)

            def v_out(i):
                act.wait_ge(v_turned, i + 1)
                act.activation(v_lat[:, :, (4 + i) * P:(5 + i) * P], bank[(0, 1, 2, 4)[i]][:].rearrange("p (c v) -> p c v", v=P), ACT.Copy).then_inc(v_read, 1)

            for j in range(16):
                hi_next(U_V, 0, j)
                if j == 0:
                    c_ktok_out(HEADS - 1)
                if j == 7:
                    for t in range(TT):
                        act.wait_ge(unit_used, U_V + j + 1)
                        act.activation(v_lat[:, t, 0:512], bank[t][:], ACT.Copy).then_inc(v_read, 1)
                if j > 8 and j % 2 == 1:
                    i = (j - 9) // 2
                    if i >= 2:
                        act.wait_ge(v_turned, i - 1)
                    act.wait_ge(unit_used, U_V + j + 1)
                    act.activation(v_cols[:, i % 2].rearrange("p (c r) -> p c r", r=ROWS), bank[4 + i][:].rearrange("p (r c) -> p c r", c=GRID_W),
                                   ACT.Copy).then_inc(vt_made, 1)
                if j in (12, 14):
                    v_out((j - 12) // 2)

            def scan_act(h, part):
                if part == 0:
                    act.wait_ge(k_turned, h + 1)
                    for d in range(2):
                        act.activation(ktok[:, 3 * d:3 * d + 3], bank[7 - d][:, 0:384].rearrange("p (a b) -> p a b", b=P), ACT.Copy).then_inc(ktok_ready, 1)
                if part == 1:
                    act.wait_ge(o_done, h + 1)
                    for c in range(TT):
                        act.activation(o_sq[:, c], bank[6][:, c * P:(c + 1) * P], ACT.Square, accum_out=stat[:, 16 + c:17 + c]).then_inc(o_root, 1)
                    act.wait_ge(o_root, 5 * h + TT)
                    act.activation(stat[:, 16:20], stat[:, 16:20], ACT.Sqrt, bias=stat[:, 63:64], scale=1.0 / P).then_inc(o_root, 1)

            def permuted(ap, scanned):
                return ap.rearrange("p (r c) -> p c r", c=GRID_W) if scanned else ap

            def straight(ap, scanned):
                return ap.rearrange("p (c r) -> p c r", r=ROWS) if scanned else ap

            def head_act(h, u0, scanned, first, scan_of):
                for j in range(8):
                    hi_next(u0, 2 * h, j)
                    if first and j in (0, 2):
                        v_out(2 + j // 2)
                    if scan_of is not None and j == 4:
                        scan_act(scan_of, 0)
                    if scan_of is not None and j == 6:
                        scan_act(scan_of, 1)
                    if j == 1:
                        act.wait_ge(unit_used, 8 * h + (u0 + j + 1))
                        if not first:
                            act.wait_ge(scores_done, 8 * (h - 1) + 1)
                        act.activation(straight(q_sb[:], scanned), permuted(bank[0][:], scanned), ACT.Copy).then_inc(proj_read, 1)
                    if j in (3, 5):
                        d = j // 2 - 1
                        act.wait_ge(unit_used, 8 * h + (u0 + j + 1))
                        act.activation(straight(sig[:, d], scanned), permuted(bank[1 + d][:], scanned), ACT.Sigmoid).then_inc(proj_read, 1)
                    if j == 7:
                        act.wait_ge(unit_used, 8 * h + (u0 + j + 1))
                        if not first:
                            act.wait_ge(head_out, h)
                        act.activation(g_sb[:], bank[3][:], ACT.Silu).then_inc(proj_read, 1)

            head_act(0, U_HEADS, False, True, None)
            with act.Fori(1, 4) as h:
                head_act(h, U_HEADS, False, False, h - 1)
            head_act(4, U_HEADS, True, False, 3)
            with act.Fori(5, HEADS) as h:
                head_act(h, U_HEADS, True, False, h - 1)

            for j in range(16):
                hi_next(U_GU, 0, j)
                if j == 4:
                    scan_act(HEADS - 1, 0)
                if j == 6:
                    scan_act(HEADS - 1, 1)
                if j % 2 == 1:
                    act.wait_ge(unit_used, U_GU + j + 1)
                    act.activation(mix[:, j // 2], bank[(j // 2) % 4][:], ACT.Gelu_apprx_tanh).then_inc(u_read, 1)

            def gv_roots(c):
                act.wait_ge(gv_step, 8 * (c + 1))
                act.activation(stat[:, 20:36], stat[:, 20:36], ACT.Sqrt, bias=stat[:, 63:64], scale=1.0 / P).then_inc(gv_root, 1)

            for j in range(16):
                hi_next(U_GV, 0, j)
                if j in (2, 6):
                    g = j // 4
                    act.wait_ge(head_out, HEADS)
                    for c in range(4):
                        act.wait_ge(row_done, 4 * g + c + 1)
                        act.activation((g1_row, g2_row)[g][:, c * 512:(c + 1) * 512], bank[4 + c][:], ACT.Copy).then_inc(row_read, 1)
                if j % 8 == 7:
                    act.wait_ge(unit_used, U_GV + j + 1)
                    for t in range(TT):
                        act.activation(gv[:, j // 8, t], bank[4 * (j // 8) + t][:], ACT.Gelu_apprx_tanh).then_inc(gv_read, 1)
                if j == 9:
                    gv_roots(0)

            def split(i):
                kt = (i + 8) % KT
                if i == 8:
                    act.wait_ge(mix_a_ready, 4)
                if i == 12:
                    act.wait_ge(mix_a_ready, 8)
                act.activation(h_hi[:, kt], mix[:, kt], ACT.Copy).then_inc(split_hi, 1)

            act.wait_ge(head_out, HEADS)
            for i in range(8):
                split(i)
            for j in range(32):
                if j == 0:
                    gv_roots(1)
                hi_next(U_OUT, 0, j)
                if j in (1, 4):
                    for i in range(4):
                        split(8 + 4 * (j // 4) + i)
            for t in range(TT):
                act.wait_ge(x_res_ready, 12 + t + 1)
                act.activation(x_norm[:, t], x_res[:, t], ACT.Square, accum_out=stat[:, 6 + t:7 + t]).then_inc(sumsq, 1)
            roots(6, TT, D)
            act.wait_ge(mod2_step, 1)
            prep(2 * KT, KT, SEQ, h_hi, lambda k: mod2[:, 2, k:k + 1], lambda k: mod2[:, 1, k:k + 1])

            act.wait_ge(prep_lo, 3 * KT)

            def hid_act(b, t):
                act.wait_ge(unit_used, 32 * b + (U_MLP + 2 * t + 2))
                if not (isinstance(b, int) and b == 0 and t < 2):
                    act.wait_ge(hid_made, HT * b + t - 1)
                act.activation(relu_sb[:, t % 2], bank[t % 4][:], ACT.Relu).then_inc(relu_made, 1)
                act.wait_ge(hid_made, HT * b + t + 1)
                act.activation(hid_hi[:, t], hid_sb[:, t % 2], ACT.Copy).then_inc(hid_hi_made, 1)

            def mlp_act(b):
                for j in range(32):
                    hi_next(U_MLP, 8 * b, j)
                    if j < 16 and j % 2 == 1:
                        hid_act(b, j // 2)

            mlp_act(0)
            with act.Fori(1, BLOCKS - 1) as b:
                mlp_act(b)
            for j in range(32):
                if j < 30:
                    hi_next(U_MLP, 8 * (BLOCKS - 1), j)
                if j < 16 and j % 2 == 1:
                    hid_act(BLOCKS - 1, j // 2)
            for t in range(TT):
                act.wait_ge(ff2_added, 16 * (BLOCKS - 1) + 12 + t + 1)
                act.activation(junk[:], x_res[:, t], ACT.Square, accum_out=stat[:, 10 + t:11 + t]).then_inc(sumsq, 1)
                act.wait_ge(sumsq, 10 + t + 1)
                act.activation(stat[:, 10 + t:11 + t], stat[:, 10 + t:11 + t], ACT.Sqrt, bias=stat[:, 63:64], scale=1.0 / D).then_inc(root, 1)

        @block.vector
        def _(dve):
            dve.memset(ones[:], 1.0).then_inc(ones_ready, 1)
            dve.memset(stat[:, 63:64], EPS).then_inc(ones_ready, 1)
            dve.memset(c_decay[:], 1.0).then_inc(ones_ready, 1)
            dve.wait_ge(small_landed, 64)
            dve.tensor_copy(mask[:], mask_f32[:]).then_inc(mask_ready, 1)
            dve.tensor_tensor(lbt[:, 0], lbl[:, 0], lbl[:, 1], ALU.max).then_inc(lb_ready, 1)
            dve.wait_ge(lb_ready, 1)
            for i in range(2):
                dve.tensor_tensor(lbt[:, 1 + i], lbl[:, i], lbt[:, 0], ALU.subtract).then_inc(lb_step, 1)
            dve.wait_ge(lb_exp, 1)
            dve.tensor_tensor(lbt[:, 0], lbt[:, 1], lbt[:, 2], ALU.add).then_inc(lb_ready, 1)
            dve.wait_ge(lb_ready, 2)
            dve.reciprocal(lbt[:, 0], lbt[:, 0]).then_inc(lb_ready, 1)
            dve.wait_ge(lb_ready, 3)
            dve.tensor_tensor(lb[:].rearrange("p a b -> p (a b)"), lbt[:, 2], lbt[:, 0], ALU.mult).then_inc(lb_ready, 1)
            dve.wait_ge(lb_ready, 4)
            dve.tensor_scalar(oml[:], lb[:], -1.0, 1.0, ALU.mult, ALU.add).then_inc(lb_ready, 1)

            def norm_rows(n_root, n0, count, dst, src, n_normed):
                dve.wait_ge(root, n_root)
                dve.reciprocal(stat[:, n0:n0 + count], stat[:, n0:n0 + count]).then_inc(rstd, 1)
                dve.wait_ge(rstd, n_root)
                for t in range(count):
                    dve.tensor_scalar(dst[:, t], src[:, t], stat[:, n0 + t:n0 + t + 1], None, ALU.mult).then_inc(normed, 1)

            def prep(n0, count, ntok, tmp, hi, lo, s, b):
                for i in range(count):
                    n = n0 + i
                    kt = n % KT
                    dve.wait_ge(prep_hi, n + 1)
                    if n >= 2:
                        dve.wait_ge(prep_lo, n - 1)
                    dve.tensor_scalar(tmp[:, n % 2, 0:ntok], bank[4 + n % 4][:, 0:ntok], s(kt), b(kt), ALU.mult, ALU.add).then_inc(prep_h, 1)
                    dve.wait_ge(prep_h, n + 1)
                    dve.tensor_tensor(lo[:, kt], tmp[:, n % 2, 0:ntok], hi[:, kt].bitcast(F32), ALU.subtract).then_inc(prep_lo, 1)

            norm_rows(1, 0, CT, ctx_tok, ctx_tok, 0)
            dve.wait_ge(ada1_done, 1)
            dve.tensor_tensor(mod1[:].rearrange("p a k c -> p (a k) c"), bank[7][:, 0:64].rearrange("p (a c) -> p a c", c=2),
                              B1_COL.unsqueeze(2).to_broadcast([P, 32, 2]), ALU.add).then_inc(mod1_ready, 1)
            dve.wait_ge(mod1_ready, 1)
            dve.tensor_scalar(mod1[:, 1], mod1[:, 1], 1.0, None, ALU.add).then_inc(mod1_step, 1)
            dve.wait_ge(mod1_step, 1)
            dve.tensor_tensor(mod1[:, 1], mod1[:, 1], N1_COL.unsqueeze(2).to_broadcast([P, KT, 2]), ALU.mult).then_inc(mod1_step, 1)
            dve.wait_ge(mod1_step, 2)
            prep(0, KT, CTX, prep_tmp, c_hi, c_lo, lambda k: mod1[:, 1, k, 1:2], lambda k: mod1[:, 0, k, 1:2])
            norm_rows(2, 2, TT, x_tok, x_tok, 2)
            prep(KT, KT, SEQ, prep_tmp, h_hi, h_lo, lambda k: mod1[:, 1, k, 0:1], lambda k: mod1[:, 0, k, 0:1])

            dve.wait_ge(prep_lo, 2 * KT)

            def c_head_dve(h, first):
                for d in range(2):
                    dve.wait_ge(cgate_read, 2 * h + d + 1)
                    if not first:
                        dve.wait_ge(c_kd_ready, 2 * h)
                    dve.tensor_scalar(c_f[:, d], c_sig[:, d], oml[:, d, bass.ds(h, 1)], lb[:, d, bass.ds(h, 1)], ALU.mult, ALU.add).then_inc(c_step, 1)
                    dve.wait_ge(c_step, 4 * h + 2 * d + 1)
                    dve.tensor_scalar(c_k[:, d], c_f[:, d], -1.0, 1.0, ALU.mult, ALU.add).then_inc(c_step, 1)
                n = CTX
                dve.tensor_tensor_scan(c_decay[:, 0, n - 2::-1], c_f[:, 0, n - 1:0:-1], c_f[:, 0, 0:n - 1], 1.0, ALU.mult, ALU.bypass).then_inc(c_scan, 1)
                dve.tensor_tensor_scan(c_decay[:, 1, 1:n], c_f[:, 1, 0:n - 1], c_f[:, 0, 0:n - 1], 1.0, ALU.mult, ALU.bypass).then_inc(c_scan, 1)
                dve.wait_ge(c_scan, 2 * h + 2)
                dve.wait_ge(c_step, 4 * h + 4)
                for d in range(2):
                    if not first:
                        dve.wait_ge(c_turned, h)
                    dve.tensor_tensor(c_kd[:, d], c_k[:, d], c_decay[:, d], ALU.mult).then_inc(c_kd_ready, 1)

            def c_state_out(h):
                dve.wait_ge(c_state_done, h + 1)
                dve.tensor_copy(s_ctx[:, bass.ds(h, 1)].rearrange("p a d v -> p (a d v)"), bank[7][:, 0:256]).then_inc(s_ctx_ready, 1)

            dve.wait_ge(ones_ready, 3)
            dve.wait_ge(mask_ready, 1)
            dve.wait_ge(lb_ready, 5)
            c_head_dve(0, True)
            with dve.Fori(1, HEADS) as h:
                c_state_out(h - 1)
                c_head_dve(h, False)
            c_state_out(HEADS - 1)

            def ada2_part(n, m):
                dve.wait_ge(ada_landed[m % 2], 64 * n + 16 * (m // 2) + 16)
                for t in range(2):
                    i = 2 * m + t
                    c = cs[:, i, 0:1]
                    if i == 0:
                        dve.tensor_scalar(ada_acc[:], ada_w[:, 0, 0], c, None, ALU.mult).then_inc(ada_summed, 1)
                    else:
                        dve.wait_ge(ada_summed, 16 * n + i)
                        dve.scalar_tensor_tensor(ada_acc[:], ada_w[:, m % 2, t], c, ada_acc[:], ALU.mult, ALU.add).then_inc(ada_summed, 1)

            mod2_flat = mod2[:].rearrange("p g k -> p (g k)")

            def ada2_take(n, b=7):
                dve.wait_ge(ada_colsum, n + 1)
                dve.tensor_tensor(mod2_flat[:, bass.ds(4 * n, 4)], bank[b][:, 508:512], B2_COL[:, bass.ds(4 * n, 4)], ALU.add).then_inc(mod2_made, 1)

            dve.wait_ge(c_kd_ready, 2 * HEADS)
            for m in range(8):
                ada2_part(0, m)
            for n in range(1, 4):
                ada2_take(n - 1, 7 if n == 1 else 3)
                for m in range(8):
                    ada2_part(n, m)

            off = [0]
            for lv in range(LEVELS + 1):
                off.append(off[-1] + (SEQ >> lv))

            def totals(lv):
                return tot[:, :, off[lv]:off[lv + 1]]

            def gates(h):
                dve.wait_ge(proj_read, 4 * h + 3)
                for d in range(2):
                    dve.tensor_scalar(tot[:, d, 0:SEQ], sig[:, d], oml[:, d, bass.ds(h, 1)], lb[:, d, bass.ds(h, 1)], ALU.mult, ALU.add).then_inc(gate_step, 1)
                dve.wait_ge(gate_step, 6 * h + 2)
                k = (yy[:, 0], xx[:, 1])
                q = (xx[:, 0], yy[:, 1])
                for d in range(2):
                    dve.tensor_scalar(k[d], tot[:, d, 0:SEQ], -1.0, 1.0, ALU.mult, ALU.add).then_inc(gate_step, 1)
                for d in range(2):
                    dve.tensor_tensor(q[d], q_sb[:], tot[:, d, 0:SEQ], ALU.mult).then_inc(gate_step, 1)
                dve.wait_ge(gate_step, 6 * h + 6)
                dve.tensor_tensor(ksum[:], k[0], k[1], ALU.add).then_inc(scan_ready, 1)

            def merge(h, i):
                b = bank[4 + i % 2][:].rearrange("p (c t) -> p c t", t=P)
                if i == 0:
                    dve.wait_ge(scores_done, 8 * h + 1)
                    dve.tensor_copy(score[:], b).then_inc(scores_merged, 1)
                else:
                    dve.copy_predicated(score[:], mask[:, i - 1].unsqueeze(1).to_broadcast([P, TT, P]), b).then_inc(scores_merged, 1)

            def grow(h, i):
                L = 1 << (i - 1)
                dve.wait_ge(scores_done, 8 * h + i + 1)
                dve.wait_ge(scores_merged, 8 * h + i)
                if i > 1:
                    dve.wait_ge(level_ready, 7 * h + i - 1)
                    dve.wait_ge(tot_ready, 7 * h + i - 1)
                else:
                    dve.wait_ge(scan_ready, h + 1)
                t = totals(i - 1).rearrange("p d (b two) -> p d b two", two=2)
                dve.tensor_tensor(totals(i), t[:, :, :, 0], t[:, :, :, 1], ALU.mult).then_inc(tot_ready, 1)
                for a, half in ((xx, 1), (yy, 0)):
                    a = a[:].rearrange("p d (b two l) -> p d b two l", two=2, l=L)
                    f = t[:, :, :, 1 - half]
                    if L == 1:
                        ins = dve.tensor_tensor(a[:, :, :, half, 0], a[:, :, :, half, 0], f, ALU.mult)
                    else:
                        ins = dve.tensor_tensor(a[:, :, :, half], a[:, :, :, half], f.unsqueeze(3).to_broadcast([P, 2, SEQ // (2 * L), L]), ALU.mult)
                ins.then_inc(level_ready, 1)

            def states(h):
                dve.wait_ge(kv_done, h + 1)
                dve.wait_ge(tot_ready, 7 * h + 7)
                for i in range(3):
                    for d in range(2):
                        c = i if d == 0 else 3 - i
                        before = s_ctx[:, bass.ds(h, 1), d].rearrange("p a v -> p (a v)") if i == 0 else state[:, d, i - 1]
                        if i:
                            dve.wait_ge(states_ready, 6 * h + 2 * (i - 1) + d + 1)
                        slot = c if d == 0 else c - 1
                        dve.scalar_tensor_tensor(state[:, d, i], before, tot[:, d, off[7] + c:off[7] + c + 1],
                                                 bank[7 - d][:, slot * P:(slot + 1) * P], ALU.mult, ALU.add).then_inc(states_ready, 1)

            def o_rows(h):
                dve.wait_ge(o_root, 5 * h + 5)
                dve.reciprocal(stat[:, 16:20], stat[:, 16:20]).then_inc(o_rstd, 1)
                dve.wait_ge(o_rstd, h + 1)
                dve.tensor_tensor(o_norm[:], bank[6][:].rearrange("p (c v) -> p c v", v=P),
                                  stat[:, 16:20].unsqueeze(2).to_broadcast([P, TT, P]), ALU.mult).then_inc(o_ready, 1)

            def head_result(h, scanned):
                dve.wait_ge(o_turned, h + 1)
                dve.wait_ge(proj_read, 4 * h + 4)
                dst = mix[:, bass.ds(h + 8, 1)].rearrange("p a t -> p (a t)")
                src, g = bank[7][:], g_sb[:]
                if scanned:
                    dst, g = (a.rearrange("p (r c) -> p c r", c=GRID_W) for a in (dst, g))
                    src = src.rearrange("p (c r) -> p c r", r=ROWS)
                dve.scalar_tensor_tensor(dst, src, OG_COL[:, bass.ds(h, 1)], g, ALU.mult, ALU.mult).then_inc(head_out, 1)

            def scan_dve(h, scanned, n, then_gates):
                ada2_take(n - 1)
                merge(h, 0)
                for i in range(1, LEVELS + 1):
                    grow(h, i)
                    merge(h, i)
                    ada2_part(n, i - 1)
                ada2_part(n, 7)
                states(h)
                o_rows(h)
                if then_gates is not None:
                    gates(then_gates)
                head_result(h, scanned)

            ada2_take(3, 3)
            for m in range(8):
                ada2_part(4, m)
            gates(0)
            with dve.Fori(1, 5) as h:
                scan_dve(h - 1, False, h + 4, h)
            with dve.Fori(5, HEADS) as h:
                scan_dve(h - 1, True, h + 4, h)
            scan_dve(HEADS - 1, True, 12, None)
            with dve.Fori(13, 16) as n:
                ada2_take(n - 1)
                for m in range(8):
                    ada2_part(n, m)
            ada2_take(15)
            dve.wait_ge(mod2_made, 16)
            dve.tensor_scalar(mod2[:, 2], mod2[:, 2], 1.0, None, ALU.add).then_inc(mod2_made, 1)
            dve.wait_ge(mod2_made, 17)
            dve.tensor_tensor(mod2[:, 2], mod2[:, 2], N2_COL, ALU.mult).then_inc(mod2_step, 1)

            rs = stat[:, 20:36].rearrange("p (t h) -> p t h", h=4)

            def gv_squares(c):
                for t in range(TT):
                    n = 8 * c + 2 * t
                    dve.wait_ge(gv_read, 4 * c + t + 1)
                    if n:
                        dve.wait_ge(gv_step, n)
                    dve.tensor_tensor(g_tmp[:, t % 2], gv[:, c, t], gv[:, c, t], ALU.mult).then_inc(gv_step, 1)
                    dve.wait_ge(gv_step, n + 1)
                    dve.tensor_reduce(rs[:, t], g_tmp[:, t % 2].rearrange("p (h d) -> p h d", d=P), AX.X, ALU.add).then_inc(gv_step, 1)

            def gv_norm(c):
                dve.wait_ge(gv_root, c + 1)
                dve.reciprocal(stat[:, 20:36], stat[:, 20:36]).then_inc(gv_rstd, 1)
                dve.wait_ge(gv_rstd, c + 1)
                for t in range(TT):
                    v = gv[:, c, t].rearrange("p (h d) -> p h d", d=P)
                    dve.tensor_tensor(v, v, rs[:, t].unsqueeze(2).to_broadcast([P, 4, P]), ALU.mult).then_inc(gv_ready, 1)

            def mixing(c):
                for i in range(4):
                    h = 4 * c + i
                    dve.wait_ge(mixed_head, h + 1)
                    if i == 0:
                        dve.wait_ge(gv_ready, 4 * c + 4)
                    if h >= 2:
                        dve.wait_ge(mix_a_ready, h - 1)
                    dve.scalar_tensor_tensor(g_tmp[:, i % 2].rearrange("p (n t) -> p n t", t=P), bank[4 * c + i][:].rearrange("p (n t) -> p n t", t=P),
                                             VG_COL[:, h:h + 1], bs[:, h].unsqueeze(1).to_broadcast([P, TT, P]), ALU.mult, ALU.add).then_inc(mixed_step, 1)
                    dve.wait_ge(mixed_step, h + 1)
                    dve.tensor_tensor(mix[:, h], mix[:, h], g_tmp[:, i % 2], ALU.mult).then_inc(mix_a_ready, 1)

            dve.wait_ge(u_read, 8)
            gv_squares(0)
            gv_norm(0)
            dve.wait_ge(ws_landed, 32)
            mixing(0)
            gv_squares(1)

            def split(i):
                kt = (i + 8) % KT
                dve.wait_ge(split_hi, i + 1)
                dve.tensor_tensor(h_lo[:, kt], mix[:, kt], h_hi[:, kt].bitcast(F32), ALU.subtract).then_inc(split_lo, 1)

            for i in range(8):
                split(i)
            gv_norm(1)
            for i in range(8, 12):
                split(i)
            mixing(1)
            for i in range(12, 16):
                split(i)

            dve.wait_ge(x_res_landed, 16 * TT)
            dve.wait_ge(row_read, 8)
            for c in range(4):
                for t in range(TT):
                    n = 4 * c + t
                    dve.wait_ge(out_done, 3 * c + t + 1) if t < 3 else dve.wait_ge(unit_used, U_OUT + 8 * (c + 1))
                    if n >= 2:
                        dve.wait_ge(x_res_ready, n - 1)
                    dve.tensor_tensor(g_tmp[:, n % 2], bank[4 * (c % 2) + t][:], g1_row[:, c * 512:(c + 1) * 512], ALU.mult).then_inc(out_tmp, 1)
                    dve.wait_ge(out_tmp, n + 1)
                    dve.tensor_tensor(x_res[:, t, c * 512:(c + 1) * 512], x_res[:, t, c * 512:(c + 1) * 512], g_tmp[:, n % 2], ALU.add).then_inc(x_res_ready, 1)
            norm_rows(3, 6, TT, x_norm, x_res, 6)
            dve.wait_ge(mod2_step, 1)
            prep(2 * KT, KT, SEQ, prep_tmp2, h_hi, h_lo, lambda k: mod2[:, 2, k:k + 1], lambda k: mod2[:, 1, k:k + 1])

            dve.wait_ge(prep_lo, 3 * KT)

            def hid(b, t):
                dve.wait_ge(relu_made, HT * b + t + 1)
                if not (isinstance(b, int) and b == 0 and t < 2):
                    dve.wait_ge(hid_ready, HT * b + t - 1)
                dve.tensor_tensor(hid_sb[:, t % 2], relu_sb[:, t % 2], relu_sb[:, t % 2], ALU.mult).then_inc(hid_made, 1)
                dve.wait_ge(hid_hi_made, HT * b + t + 1)
                dve.tensor_tensor(hid_lo[:, t], hid_sb[:, t % 2], hid_hi[:, t].bitcast(F32), ALU.subtract).then_inc(hid_ready, 1)

            def second_residual(b, c, t):
                n = 4 * c + t
                dve.wait_ge(ff2_done, 12 * b + (3 * c + t + 1)) if t < 3 else dve.wait_ge(unit_used, 32 * b + (U_MLP + 16 + 4 * (c + 1)))
                if not (isinstance(b, int) and b == 0 and n < 2):
                    dve.wait_ge(ff2_added, 16 * b + n - 1)
                dve.tensor_tensor(g_tmp[:, n % 2], bank[4 * (1 - c % 2) + t][:], g2_row[:, c * 512:(c + 1) * 512], ALU.mult).then_inc(ff2_tmp, 1)
                dve.wait_ge(ff2_tmp, 16 * b + n + 1)
                dve.tensor_tensor(x_res[:, t, c * 512:(c + 1) * 512], x_res[:, t, c * 512:(c + 1) * 512], g_tmp[:, n % 2], ALU.add).then_inc(ff2_added, 1)

            def mlp_dve(b):
                for t in range(HT):
                    hid(b, t)
                for c in range(4):
                    for t in range(TT):
                        second_residual(b, c, t)

            mlp_dve(0)
            with dve.Fori(1, BLOCKS) as b:
                mlp_dve(b)
            dve.wait_ge(fin_landed, 16)
            for t in range(TT):
                dve.wait_ge(root, 4 + t)
                dve.reciprocal(stat[:, 10 + t:11 + t], stat[:, 10 + t:11 + t]).then_inc(rstd, 1)
                dve.wait_ge(rstd, 4 + t)
                dve.scalar_tensor_tensor(x_res[:, t], x_res[:, t], stat[:, 10 + t:11 + t], fin_row[:], ALU.mult, ALU.mult).then_inc(fin_ready, 1)

        @block.tensor
        def _(pe):
            pe.wait_ge(cs_ready, 1)

            def ada1(i, s, first):
                pe.wait_ge(ada1_landed[s], 16 * i + 16)
                for j in range(32):
                    mm = pe.matmul(bank[7][:, 2 * j:2 * j + 2], ada1_w[:, s, j * P:(j + 1) * P], cs[:, bass.ds(4 * i + s, 1)].rearrange("p a c -> p (a c)"),
                                   start=(first and s == 0 and j == 0), stop=(isinstance(i, int) and 4 * i + s == KT - 1 and j == 31),
                                   skip_group_check=True)
                return mm

            for s in range(4):
                ada1(0, s, True).then_inc(ada1_used, 1)
            with pe.Fori(1, KT // 4 - 1) as i:
                for s in range(4):
                    ada1(i, s, False).then_inc(ada1_used, 1)
            for s in range(4):
                mm = ada1(KT // 4 - 1, s, False)
                mm.then_inc(ada1_used if s < 3 else ada1_done, 1)

            def prep(n0, count, src, ntile, n_normed):
                for i in range(count):
                    n = n0 + i
                    kt = n % KT
                    if n % KT == 0:
                        pe.wait_ge(normed, n_normed)
                    if n >= 4:
                        pe.wait_ge(prep_h, n - 3)
                    for t in range(ntile):
                        mm = pe.transpose(bank[4 + n % 4][:, t * P:(t + 1) * P], src[:, t, kt * P:(kt + 1) * P], ident[:])
                    mm.then_inc(turned, 1)

            pe.wait_ge(mod1_ready, 1)
            prep(0, KT, ctx_tok, CT, CT)

            def tall(r, half, dst, hi, lo, between=(None, None)):
                for k in range(8):
                    if k % 4 == 0 and between[k // 4] is not None:
                        between[k // 4]()
                    kt = 8 * half + k
                    wh, wl = w_hi[:, r % 2, k * P:(k + 1) * P], w_lo[:, r % 2, k * P:(k + 1) * P]
                    pe.matmul(dst, wh, hi[:, kt], start=(kt == 0), stop=False)
                    pe.matmul(dst, wh, lo[:, kt], start=False, stop=False)
                    mm = pe.matmul(dst, wl, hi[:, kt], start=False, stop=(kt == KT - 1))
                return mm

            def wide(r, kts, first, last, banks, hi, lo, tokens, wait_tile=None):
                mms = []
                for k in range(2):
                    if wait_tile is not None:
                        wait_tile(k)
                    for t, b in enumerate(banks):
                        xh, xl = tokens(hi, kts[k], t), tokens(lo, kts[k], t)
                        wh, wl = w_hi[:, r % 2, k * 512:(k + 1) * 512], w_lo[:, r % 2, k * 512:(k + 1) * 512]
                        pe.matmul(b[:], xh, wh, start=(first and k == 0), stop=False)
                        pe.matmul(b[:], xh, wl, start=False, stop=False)
                        mm = pe.matmul(b[:], xl, wh, start=False, stop=(last and k == 1))
                        if last and k == 1:
                            mms.append(mm)
                return mm, mms

            def raster(a, kt, t):
                return a[:, kt, t * P:(t + 1) * P]

            for j in range(16):
                pe.wait_ge(lo_done, U_CTX_V + j + 1)
                c, i = j // 8, j % 8
                if c == 0:
                    pe.wait_ge(prep_lo, 2 * i + 2)
                mm, _ = wide(j % 4, (2 * i, 2 * i + 1), i == 0, i == 7, bank[2 * c:2 * c + 2], c_hi, c_lo, raster)
                mm.then_inc(unit_used, 1)
                if j >= 8:
                    prep(KT + 2 * (j - 8), 2, x_tok, TT, CT + TT)

            def c_turn(h):
                pe.wait_ge(c_kd_ready, 2 * h + 2)
                for d in range(2):
                    for t in range(CT):
                        mm = pe.transpose(bank[6][:, (2 * d + t) * P:(2 * d + t + 1) * P], c_kd[:, d, t * P:(t + 1) * P], ident[:])
                mm.then_inc(c_turned, 1)

            def c_states(h):
                pe.wait_ge(c_ktok_ready, h + 1)
                for d in range(2):
                    for t in range(CT):
                        mm = pe.matmul(bank[7][:, d * P:(d + 1) * P], c_ktok[:, 2 * d + t], v_ctx[:, t, bass.ds(P * h, P)], start=(t == 0), stop=(t == CT - 1))
                mm.then_inc(c_state_done, 1)

            def c_head_pe(h, first):
                for j in range(4):
                    pe.wait_ge(lo_done, 4 * h + (U_CTX_HEADS + j + 1))
                    d = j // 2
                    if j % 2 == 0 and not first:
                        pe.wait_ge(cgate_read, 2 * h - 1 + d)
                    if j == 1 and not first:
                        c_turn(h - 1)
                    if j == 3 and not first:
                        c_states(h - 1)
                    tall(j, j % 2, bank[d][:, 0:CTX], c_hi, c_lo).then_inc(unit_used, 1)

            pe.wait_ge(cv_read, 4)
            pe.wait_ge(prep_lo, 2 * KT)
            c_head_pe(0, True)
            with pe.Fori(1, HEADS) as h:
                c_head_pe(h, False)

            def ada2_colsum(n, b=7):
                pe.wait_ge(ada_summed, 16 * n + 16)
                for i in range(4):
                    mm = pe.matmul(bank[b][:, 508 + i:509 + i], ada_acc[:, i * P:(i + 1) * P], ones[:, 0:1], start=True, stop=True)
                mm.then_inc(ada_colsum, 1)

            V_BANK = (0, 1, 2, 4)

            def v_turn_pe(i):
                pe.wait_ge(vt_made, i + 1)
                pe.wait_ge(v_read, 4)
                for c in range(TT):
                    mm = pe.transpose(bank[V_BANK[i]][:, c * P:(c + 1) * P], v_cols[:, i % 2, c * P:(c + 1) * P], ident[:])
                mm.then_inc(v_turned, 1)

            for j in range(16):
                pe.wait_ge(lo_done, U_V + j + 1)
                c, i = j // 8, j % 8
                if i == 0 and c == 0:
                    pe.wait_ge(cgate_read, 2 * HEADS)
                if j == 8:
                    pe.wait_ge(mod2_made, 1)
                if c == 0:
                    mm, _ = wide(j % 4, (2 * i, 2 * i + 1), i == 0, i == 7, bank[0:4], h_hi, h_lo, raster)
                else:
                    mm = tall(j % 4, j % 2, bank[4 + i // 2][:], h_hi, h_lo)
                mm.then_inc(unit_used, 1)
                if j in (11, 13, 15):
                    v_turn_pe((j - 11) // 2)
                if j == 1:
                    c_turn(HEADS - 1)
                if j == 3:
                    c_states(HEADS - 1)
                if j == 4:
                    pe.wait_ge(s_ctx_ready, HEADS)
                    ada2_colsum(0)
                if j == 8:
                    pe.wait_ge(v_read, 4)
                    ada2_colsum(1, 3)
                if j == 12:
                    pe.wait_ge(mod2_made, 2)
                    ada2_colsum(2, 3)

            def half_of(a, i, chunk, second):
                v = a[:, chunk * P:(chunk + 1) * P].rearrange("p (b two l) -> p b two l", two=2, l=1 << (i - 1))
                v = v[:, :, 1 if second else 0]
                return v[:, :, 0] if i == 1 else (v[:, 0] if i == LEVELS else v)

            def step(h, i):
                if i <= LEVELS:
                    b = bank[4 + i % 2]
                    if i == 0:
                        pe.wait_ge(scan_ready, h + 1)
                    if i >= 2:
                        pe.wait_ge(level_ready, 7 * h + i - 1)
                        pe.wait_ge(scores_merged, 8 * h + i - 1)
                    for c in range(TT):
                        whole = slice(c * P, (c + 1) * P)
                        if i == 0:
                            mm = pe.matmul(b[:, whole], ksum[:, whole], q_sb[:, whole], start=True, stop=True)
                        else:
                            pe.matmul(half_of(b, i, c, True), yy[:, 0, whole], half_of(xx[:, 0], i, c, True), start=True, stop=True)
                            mm = pe.matmul(half_of(b, i, c, False), xx[:, 1, whole], half_of(yy[:, 1], i, c, False), start=True, stop=True)
                    mm.then_inc(scores_done, 1)
                elif i == 8:
                    pe.wait_ge(level_ready, 7 * h + 7)
                    for c in range(3):
                        pe.transpose(bank[7][:, c * P:(c + 1) * P], yy[:, 0, c * P:(c + 1) * P], ident[:])
                        mm = pe.transpose(bank[6][:, c * P:(c + 1) * P], xx[:, 1, (c + 1) * P:(c + 2) * P], ident[:])
                    mm.then_inc(k_turned, 1)
                elif i == 9:
                    pe.wait_ge(ktok_ready, 2 * h + 2)
                    for c in range(3):
                        pe.matmul(bank[7][:, c * P:(c + 1) * P], ktok[:, c], v_lat[:, c, bass.ds(P * h, P)], start=True, stop=True)
                        mm = pe.matmul(bank[6][:, c * P:(c + 1) * P], ktok[:, 3 + c], v_lat[:, c + 1, bass.ds(P * h, P)], start=True, stop=True)
                    mm.then_inc(kv_done, 1)
                elif i == 10:
                    pe.wait_ge(states_ready, 6 * h + 6)
                    pe.wait_ge(scores_merged, 8 * h + 8)
                    for c in range(TT):
                        whole = slice(c * P, (c + 1) * P)
                        ctx_state = lambda d: s_ctx[:, bass.ds(h, 1), d].rearrange("p a v -> p (a v)")
                        sf = ctx_state(0) if c == 0 else state[:, 0, c - 1]
                        sb = ctx_state(1) if c == 3 else state[:, 1, 2 - c]
                        pe.matmul(bank[6][:, whole], score[:, c], v_lat[:, c, bass.ds(P * h, P)], start=True, stop=False)
                        pe.matmul(bank[6][:, whole], xx[:, 0, whole], sf, start=False, stop=False)
                        mm = pe.matmul(bank[6][:, whole], yy[:, 1, whole], sb, start=False, stop=True)
                    mm.then_inc(o_done, 1)
                else:
                    pe.wait_ge(o_ready, h + 1)
                    for c in range(TT):
                        mm = pe.transpose(bank[7][:, c * P:(c + 1) * P], o_norm[:, c], ident[:])
                    mm.then_inc(o_turned, 1)

            def steps(h, slot):
                if h is None or slot not in STEP_SLOTS:
                    return None

                def run():
                    for i in STEP_SLOTS[slot]:
                        step(h, i)
                return run

            def head_pe(h, first, scan_of):
                for j in range(8):
                    pe.wait_ge(lo_done, 8 * h + (U_HEADS + j + 1))
                    b = j // 2
                    if j % 2 == 0 and not first:
                        pe.wait_ge(proj_read, 4 * (h - 1) + b + 1)
                    if first and j in (0, 2, 4):
                        pe.wait_ge(v_read, 5 + b)
                    if first and j == 6:
                        pe.wait_ge(mod2_made, 4)
                    mm = tall(j % 4, j % 2, bank[b][:], h_hi, h_lo, (steps(scan_of, 2 * j), steps(scan_of, 2 * j + 1)))
                    mm.then_inc(unit_used, 1)
                    if first and j == 1:
                        v_turn_pe(3)
                    if first and j == 0:
                        pe.wait_ge(mod2_made, 3)
                        ada2_colsum(3, 3)
                if not first:
                    pe.wait_ge(head_out, scan_of + 1)
                ada2_colsum(h + 4)

            head_pe(0, True, None)
            with pe.Fori(1, HEADS) as h:
                head_pe(h, False, h - 1)

            for j in range(16):
                pe.wait_ge(lo_done, U_GU + j + 1)
                b = j // 2
                if j % 2 == 0:
                    if b < 4:
                        pe.wait_ge(proj_read, 4 * (HEADS - 1) + b + 1)
                    else:
                        pe.wait_ge(u_read, b - 3)
                last_scan = HEADS - 1 if j < 8 else None
                mm = tall(j % 4, j % 2, bank[b % 4][:], h_hi, h_lo, (steps(last_scan, 2 * j), steps(last_scan, 2 * j + 1)))
                mm.then_inc(unit_used, 1)
                if j == 8:
                    pe.wait_ge(head_out, HEADS)
                    ada2_colsum(12)
                if j == 12:
                    pe.wait_ge(mod2_made, 13)
                    ada2_colsum(13)

            def gate_row(g):
                for c in range(4):
                    for i in range(4):
                        k = 4 * c + i
                        src = mod2[:, 3 * g, k:k + 1].to_broadcast([P, P])
                        mm = pe.matmul(bank[4 + c][:, i * P:(i + 1) * P], src, ident[:], start=True, stop=True)
                    mm.then_inc(row_done, 1)

            def mix_heads(c):
                pe.wait_ge(ws_landed, 32)
                pe.wait_ge(gv_ready, 4 * c + 4)
                for i in range(4):
                    for n in range(TT):
                        mm = pe.matmul(bank[4 * c + i][:, n * P:(n + 1) * P], gv[:, c, n, i * P:(i + 1) * P], ws[:, 4 * c + i], start=True, stop=True)
                    mm.then_inc(mixed_head, 1)

            for j in range(16):
                pe.wait_ge(lo_done, U_GV + j + 1)
                c, i = j // 8, j % 8
                if j == 0:
                    pe.wait_ge(u_read, 8)
                if j == 8:
                    pe.wait_ge(row_read, 8)
                mm, _ = wide(j % 4, (2 * i, 2 * i + 1), i == 0, i == 7, bank[4 * c:4 * c + 4], h_hi, h_lo, raster)
                mm.then_inc(unit_used, 1)
                if j == 0:
                    pe.wait_ge(mod2_made, 14)
                    ada2_colsum(14)
                if j == 1:
                    pe.wait_ge(mod2_made, 15)
                    gate_row(0)
                if j == 4:
                    pe.wait_ge(row_read, 4)
                    ada2_colsum(15)
                if j == 5:
                    pe.wait_ge(mod2_made, 16)
                    gate_row(1)
                if j == 11:
                    mix_heads(0)

            for j in range(32):
                pe.wait_ge(lo_done, U_OUT + j + 1)
                c, i = j // 8, j % 8
                if i == 0:
                    if c == 0:
                        pe.wait_ge(mixed_step, 4)
                    elif c == 1:
                        pe.wait_ge(mixed_step, 8)
                    else:
                        pe.wait_ge(out_tmp, 4 * (c - 1))
                if j == 4:
                    pe.wait_ge(gv_read, 8)
                    mix_heads(1)
                order = [(2 * i + k + 8) % KT for k in range(2)]
                tile_ready = (lambda k, i=i: pe.wait_ge(split_lo, 2 * i + k + 1)) if c == 0 else None
                mm, mms = wide(j % 4, order, i == 0, i == 7, bank[4 * (c % 2):4 * (c % 2) + 4], h_hi, h_lo, raster, tile_ready)
                for m in mms[:-1]:
                    m.then_inc(out_done, 1)
                mm.then_inc(unit_used, 1)

            pe.wait_ge(out_tmp, 16)
            prep(2 * KT, KT, x_norm, TT, CT + 2 * TT)

            def mlp_pe(b, first):
                for j in range(16):
                    pe.wait_ge(lo_done, 32 * b + (U_MLP + j + 1))
                    t = j // 2
                    if j % 2 == 0:
                        if t < 4:
                            if not first:
                                pe.wait_ge(ff2_tmp, 16 * (b - 1) + 12 + t + 1)
                        else:
                            pe.wait_ge(relu_made, HT * b + t - 3)
                    if first and j < 2:
                        for k in range(8):
                            kt = 8 * j + k
                            pe.wait_ge(prep_lo, 2 * KT + kt + 1)
                            wh, wl = w_hi[:, j % 2, k * P:(k + 1) * P], w_lo[:, j % 2, k * P:(k + 1) * P]
                            pe.matmul(bank[0][:], wh, h_hi[:, kt], start=(kt == 0), stop=False)
                            pe.matmul(bank[0][:], wh, h_lo[:, kt], start=False, stop=False)
                            mm = pe.matmul(bank[0][:], wl, h_hi[:, kt], start=False, stop=(kt == KT - 1))
                    else:
                        mm = tall(j % 4, j % 2, bank[t % 4][:], h_hi, h_lo)
                    mm.then_inc(unit_used, 1)
                for j in range(16):
                    pe.wait_ge(lo_done, 32 * b + (U_MLP + 16 + j + 1))
                    c, i = j // 4, j % 4
                    banks = bank[4:8] if c % 2 == 0 else bank[0:4]
                    if i == 0:
                        if c == 0:
                            if not first:
                                pe.wait_ge(ff2_tmp, 16 * (b - 1) + 12)
                        elif c == 1:
                            pe.wait_ge(relu_made, HT * b + HT)
                        else:
                            pe.wait_ge(ff2_tmp, 16 * b + 4 * (c - 1))
                    tile_ready = (lambda k, i=i: pe.wait_ge(hid_ready, HT * b + 2 * i + k + 1)) if c == 0 else None
                    mm, mms = wide(j % 4, (2 * i, 2 * i + 1), i == 0, i == 3, banks, hid_hi, hid_lo, raster, tile_ready)
                    for m in mms[:-1]:
                        m.then_inc(ff2_done, 1)
                    mm.then_inc(unit_used, 1)

            mlp_pe(0, True)
            with pe.Fori(1, BLOCKS) as b:
                mlp_pe(b, False)


def tall_units(w):
    n = w.shape[1] // P
    return w.reshape(2, 8, P, n, P).transpose(3, 0, 2, 1, 4).reshape(2 * n, P, UNIT)


def wide_units(w):
    k, n = w.shape[0] // (2 * P), w.shape[1] // 512
    return w.reshape(k, 2, P, n, 512).transpose(3, 0, 2, 1, 4).reshape(n * k, P, UNIT)


def kernel(**inputs):
    import numpy as np
    import concourse.bacc as bacc
    from concourse.bass_utils import run_bass_kernel_spmd as run

    a = {k: np.asarray(v) for k, v in inputs.items()}
    w_in, w_out, w1, w2 = a["w_in"][0], a["w_out"][0], a["w_ff1"][0], a["w_ff2"][0]
    U, V, Q, I, FF, FB, G = (w_in[:, 1024 * i:1024 * (i + 1)] for i in range(7))

    def tile(w, h):
        return w[:, h * P:(h + 1) * P]

    parts = [wide_units(I)]
    for h in range(HEADS):
        parts += [tall_units(tile(FF, h)), tall_units(tile(FB, h))]
    parts += [wide_units(I[:, :512]), tall_units(I[:, 512:])]
    for h in range(HEADS):
        parts += [tall_units(tile(w, h)) for w in (Q, FF, FB, G)]
    parts += [tall_units(U), wide_units(V), wide_units(np.concatenate([w_out[1024:], w_out[:1024]], 0))]
    for b in range(BLOCKS):
        s = slice(1024 * b, 1024 * (b + 1))
        parts += [tall_units(w1[:, s]), wide_units(w2[s])]
    stream = np.concatenate(parts, 0)
    assert stream.shape[0] == UNITS

    def columns(v):
        return v.reshape(-1, P).T

    b_ada = a["b_ada"][0]
    cond = np.stack([columns(a["c"][0]), columns(a["c_ctx"])], 2).reshape(P, 2 * KT)
    cols = np.concatenate([cond, columns(b_ada), columns(a["norm1_gain"][0]), columns(a["norm2_gain"][0]),
                           a["gmlp_v_gain"][0].T, a["hgrn_o_gain"][0].T, np.zeros((P, 16), np.float32)], 1)
    small = a["hgrn_lb_logits"].reshape(2, 2, HEADS, P).transpose(3, 0, 1, 2).reshape(P, 4 * HEADS)
    t = np.arange(P)
    mask = np.stack([((t[:, None] >> i) == (t[None, :] >> i) ^ 1) for i in range(LEVELS)], 1).astype(np.float32)
    arrays = {
        "ctx_x": a["ctx"][0], "x": a["x"][0], "w_stream": stream, "w_ada": a["w_ada"][0], "cols": cols, "small": small,
        "ident": np.eye(P, dtype=np.float32), "mask": mask, "bs_row": a["gmlp_b_s"][0], "final_row": a["final_gain"],
        "ws_t": a["gmlp_w_s"][0].transpose(2, 0, 1),
    }
    arrays = {f"in_{k}": np.ascontiguousarray(v) for k, v in arrays.items()}
    nc = bacc.Bacc("TRN2", target_bir_lowering=False, num_devices=1)
    ap = {k[3:]: nc.dram_tensor(k, v.shape, mybir.dt.from_np(v.dtype), kind="ExternalInput").ap() for k, v in arrays.items()}
    out = nc.dram_tensor("out", (SEQ, D), F32, kind="ExternalOutput").ap()
    build(nc, ap["ctx_x"], ap["x"], ap["w_stream"], ap["w_ada"], ap["cols"], ap["small"], (ap["ident"], ap["mask"]),
          ap["bs_row"], ap["final_row"], ap["ws_t"], out)
    return run(nc, [arrays], core_ids=[0]).results[0]["out"].reshape(1, SEQ, D)
```

```python
from contextlib import ExitStack

import concourse.bass as bass
from concourse import mybir

F32 = mybir.dt.float32
F32R = mybir.dt.float32r
U8 = mybir.dt.uint8
ACT = mybir.ActivationFunctionType
ALU = mybir.AluOpType
AX = mybir.AxisListType

P = 128
D = 2048
KT = D // P
SEQ, CTX = 512, 256
TT, CT = SEQ // P, CTX // P
HEADS = 8
ROWS, GRID_W = 8, 64
DFF = 8192
BLOCKS = 8
HT = DFF // BLOCKS // P
UNIT = 1024
LEVELS = 7
EPS = 1e-6
KB = 1024

U_CTX_V = 0
U_CTX_HEADS = U_CTX_V + 16
U_V = U_CTX_HEADS + 4 * HEADS
U_HEADS = U_V + 16
U_GU = U_HEADS + 8 * HEADS
U_GV = U_GU + 16
U_OUT = U_GV + 16
U_MLP = U_OUT + 32
UNITS = U_MLP + 32 * BLOCKS

DVE_CUTS = U_CTX_HEADS + 2

STEP_SLOTS = {0: [0, 1], 1: [2], 2: [3], 4: [4], 5: [5], 6: [6], 7: [7], 8: [8], 10: [9], 12: [10], 15: [11]}


def build(nc, ctx_x, x, w_stream, w_ada, cols, small, masks, bs_row, final_row, ws_t, out):
    with ExitStack() as stack:
        base = nc.sbuf_base
        top = nc.sbuf_usable_end
        where = [base + (-base) % 32]

        def fixed(name, shape, dt=F32):
            n = 1 if dt == U8 else 4
            for s in shape[1:]:
                n *= s
            t = nc.alloc_sbuf_tensor_at(name, shape, dt, offset=where[0])
            where[0] += n + (-n) % 32
            return t

        raw = fixed("raw", [P, 4, UNIT])
        w_hi = fixed("w_hi", [P, 2, UNIT], F32R)
        w_lo = fixed("w_lo", [P, 2, UNIT], F32R)
        r1 = where[0]
        h_hi = fixed("h_hi", [P, KT, SEQ], F32R)
        h_lo = fixed("h_lo", [P, KT, SEQ], F32R)
        ada1_w = nc.alloc_sbuf_tensor_at("ada1_w", [P, 4, 4096], F32, offset=r1)
        junk = nc.alloc_sbuf_tensor_at("junk", [P, D], F32, offset=r1)
        ident = fixed("ident", [P, P])
        ones = fixed("ones", [P, 8])
        mask = fixed("mask", [P, LEVELS, P], U8)
        col = fixed("col", [P, 192])
        cs = fixed("cs", [P, KT, 2])
        mod1 = fixed("mod1", [P, 2, KT, 2])
        mod2 = fixed("mod2", [P, 4, KT])
        lb = fixed("lb", [P, 2, HEADS])
        oml = fixed("oml", [P, 2, HEADS])
        lbt = fixed("lbt", [P, 3, 2 * HEADS])
        stat = fixed("stat", [P, 64])
        w0 = where[0]
        assert w0 + 108 * KB <= top, (w0, top)

        def work(name, kb, shape, dt=F32):
            return nc.alloc_sbuf_tensor_at(name, shape, dt, offset=w0 + int(kb * KB))

        C_COL = col[:, 0:32].rearrange("p (k c) -> p k c", c=2)
        B1_COL = col[:, 32:64]
        B2_COL = col[:, 64:128]
        N1_COL, N2_COL = col[:, 128:144], col[:, 144:160]
        VG_COL, OG_COL = col[:, 160:168], col[:, 168:176]
        lbl = fixed("lbl", [P, 2, 2 * HEADS])
        w0 = where[0]
        assert w0 + 108 * KB <= top, (w0, top)

        c_hi = work("c_hi", 0, [P, KT, CTX], F32R)
        c_lo = work("c_lo", 16, [P, KT, CTX], F32R)
        ada1_row = work("ada1_row", 0, [2, 7, 512])
        ada1_acc = work("ada1_acc", 16, [P, 2, 512])
        ctx_tok = work("ctx_tok", 32, [P, CT, D])
        v_ctx = work("v_ctx", 48, [P, CT, 1024])
        x_tok = work("x_tok", 56, [P, TT, D])
        prep_tmp = work("prep_tmp", 88, [P, 2, SEQ])
        c_sig = work("c_sig", 88, [P, 2, CTX])
        c_f = work("c_f", 90, [P, 2, CTX])
        c_k = work("c_k", 92, [P, 2, CTX])
        c_decay = work("c_decay", 94, [P, 2, CTX])
        c_kd = work("c_kd", 96, [P, 2, CTX])
        c_ktok = work("c_ktok", 98, [P, 4, P])
        mask_f32 = work("mask_f32", 100, [P, LEVELS, P])
        s_ctx = work("s_ctx", 100, [P, HEADS, 2, P])
        v_lat = work("v_lat", 0, [P, TT, 1024])
        v_cols = work("v_cols", 16, [P, 2, SEQ])
        mix = work("mix", 16, [P, KT, SEQ])
        q_sb = work("q_sb", 48, [P, SEQ])
        sig = work("sig", 50, [P, 2, SEQ])
        g_sb = work("g_sb", 54, [P, SEQ])
        tot = work("tot", 56, [P, 2, 1024])
        kq = work("kq", 64, [P, 4, SEQ])
        yy = kq[:, 0:2]
        xx = kq[:, 2:4]
        k_meet = work("k_meet", 97, [P, SEQ])
        q_meet = work("q_meet", 95, [P, SEQ])
        ksum = work("ksum", 72, [P, SEQ])
        score = work("score", 74, [P, TT, P])
        ktok = work("ktok", 76, [P, 6, P])
        state = work("state", 79, [P, 2, 3, P])
        o_norm = work("o_norm", 82, [P, TT, P])
        ada_w = work("ada_w", 85, [P, 2, 2, 512])
        ada_acc = work("ada_acc", 93, [P, 512])
        gv = work("gv", 0, [P, 2, TT, 512])
        g1_row = work("g1_row", 48, [P, D])
        g2_row = work("g2_row", 56, [P, D])
        g_tmp = work("g_tmp", 64, [P, 2, 512])
        x_res = work("x_res", 68, [P, TT, D])
        ws = work("ws", 100, [P, HEADS, P])
        bs = work("bs", 104, [P, HEADS, P])
        ada_w2 = work("ada_w2", 56, [P, 2, 2, 512])
        ada_acc2 = work("ada_acc2", 8, [P, 512])
        relu_sb = work("relu_sb", 0, [P, 2, SEQ])
        hid_sb = work("hid_sb", 4, [P, 2, SEQ])
        fin_row = work("fin_row", 8, [P, D])
        x_norm = work("x_norm", 16, [P, TT, D])
        hid_hi = work("hid_hi", 16, [P, HT, SEQ], F32R)
        hid_lo = work("hid_lo", 32, [P, HT, SEQ], F32R)
        prep_tmp2 = work("prep_tmp2", 0, [P, 2, SEQ])

        bank = [stack.enter_context(nc.psum_tensor(f"bank{i}", [P, 512], F32)) for i in range(8)]

        def sem(name):
            return stack.enter_context(nc.semaphore(name))

        raw_landed = [sem(f"raw_landed{i}") for i in range(4)]
        hi_done, lo_done, unit_used = sem("hi_done"), sem("lo_done"), sem("unit_used")
        cols_landed = sem("cols_landed")
        small_landed, ctx_landed, x_landed = sem("small_landed"), sem("ctx_landed"), sem("x_landed")
        ada1_landed = [sem(f"ada1_landed{i}") for i in range(4)]
        ada1_used, ada1_done = sem("ada1_used"), sem("ada1_done")
        ada1_rows, ada1_cols, ada1_summed = sem("ada1_rows"), sem("ada1_cols"), sem("ada1_summed")
        cs_ready, ones_ready, mod1_ready, mod1_step = sem("cs_ready"), sem("ones_ready"), sem("mod1_ready"), sem("mod1_step")
        lb_step, lb_exp, lb_ready = sem("lb_step"), sem("lb_exp"), sem("lb_ready")
        mask_ready = sem("mask_ready")
        sumsq, root, rstd, normed, normed_act = sem("sumsq"), sem("root"), sem("rstd"), sem("normed"), sem("normed_act")
        turned, prep_hi, prep_h, prep_lo = sem("turned"), sem("prep_hi"), sem("prep_h"), sem("prep_lo")
        cv_read = sem("cv_read")
        c_scan = sem("c_scan")
        cgate_read, c_step, c_kd_ready = sem("cgate_read"), sem("c_step"), sem("c_kd_ready")
        c_turned, c_ktok_ready, c_state_done, s_ctx_ready = sem("c_turned"), sem("c_ktok_ready"), sem("c_state_done"), sem("s_ctx_ready")
        vt_made, v_turned = sem("vt_made"), sem("v_turned")
        v_read, proj_read = sem("v_read"), sem("proj_read")
        gate_step, scan_ready = sem("gate_step"), sem("scan_ready")
        scores_done, scores_merged, level_ready, tot_ready = sem("scores_done"), sem("scores_merged"), sem("level_ready"), sem("tot_ready")
        decayed = sem("decayed")
        k_turned, ktok_ready, kv_done, states_ready = sem("k_turned"), sem("ktok_ready"), sem("kv_done"), sem("states_ready")
        o_done, o_root, o_rstd, o_ready, o_turned, head_out = sem("o_done"), sem("o_root"), sem("o_rstd"), sem("o_ready"), sem("o_turned"), sem("head_out")
        ada_landed = [sem(f"ada_landed{i}") for i in range(2)]
        ada_summed, ada_colsum, mod2_made, mod2_step = sem("ada_summed"), sem("ada_colsum"), sem("mod2_made"), sem("mod2_step")
        row_done, row_read = sem("row_done"), sem("row_read")
        u_read, gv_read = sem("u_read"), sem("gv_read")
        gv_step, gv_root, gv_ready, ws_landed = sem("gv_step"), sem("gv_root"), sem("gv_ready"), sem("ws_landed")
        gv_rstd, mixed_head = sem("gv_rstd"), sem("mixed_head")
        mixed_step, mix_a_ready = sem("mixed_step"), sem("mix_a_ready")
        split_hi, split_lo, x_res_landed = sem("split_hi"), sem("split_lo"), sem("x_res_landed")
        out_done, out_tmp, x_res_ready = sem("out_done"), sem("out_tmp"), sem("x_res_ready")
        relu_made, hid_made, hid_hi_made, hid_ready = sem("relu_made"), sem("hid_made"), sem("hid_hi_made"), sem("hid_ready")
        part_squared, total_squared = sem("part_squared"), sem("total_squared")
        ff2_done, ff2_tmp, ff2_added = sem("ff2_done"), sem("ff2_tmp"), sem("ff2_added")
        fin_landed, fin_ready, stored = sem("fin_landed"), sem("fin_ready"), sem("stored")

        block = stack.enter_context(nc.Block())

        @block.sync
        def _(sp):
            def load_ada1(i, s, first):
                if not first:
                    sp.wait_ge(ada1_used, 4 * (i - 1) + s + 1)
                    sp.wait_ge(ada1_summed, 8 * (i - 1) + 2 * s + 2)
                sp.dma_start(ada1_w[:, s], w_ada[(4 * i + s) * P:(4 * i + s + 1) * P, 0:4096]).then_inc(ada1_landed[s], 16)

            sp.dma_start(col[:], cols).then_inc(cols_landed, 16)
            for s in range(4):
                load_ada1(0, s, True)
                if s == 1:
                    for t in range(CT):
                        sp.dma_start(ctx_tok[:, t], ctx_x[t * P:(t + 1) * P, :]).then_inc(ctx_landed, 16)
            for i in range(1, KT // 4):
                for s in range(4):
                    load_ada1(i, s, False)

            def load_unit(q, r, first=False):
                if not first:
                    sp.wait_ge(lo_done, 4 * (q - 1) + r + 1)
                sp.dma_start(raw[:, r], w_stream[bass.ds(4 * q + r, 1)].rearrange("a p n -> (a p) n")).then_inc(raw_landed[r], 16)

            def load_ada2(n, m, dst=ada_w):
                if not (isinstance(n, int) and n == 0 and m < 2):
                    sp.wait_ge(ada_summed, 16 * n + 2 * m - 2)
                src = w_ada[2 * m * P:(2 * m + 2) * P, bass.ds(4096 + 512 * n, 512)]
                sp.dma_start(dst[:, m % 2], src.rearrange("(t p) c -> p t c", p=P)).then_inc(ada_landed[m % 2], 16)

            for r in range(4):
                load_unit(0, r, True)
            sp.wait_ge(sumsq, CT)
            for t in range(TT):
                sp.dma_start(x_tok[:, t], x[t * P:(t + 1) * P, :]).then_inc(x_landed, 16)
            with sp.Fori(1, U_V // 4) as q:
                for r in range(4):
                    load_unit(q, r)

            for r in range(4):
                load_unit(U_V // 4, r)
            sp.wait_ge(c_kd_ready, 2 * HEADS)
            for r in range(4):
                load_unit(U_V // 4 + 1, r)
                for m in ((0, 1), (2, 3), (4,), (5,))[r]:
                    load_ada2(0, m)
            with sp.Fori(1, 12) as n:
                for r in range(8):
                    load_unit(2 * n + (U_V // 4 + r // 4), r % 4)
                    load_ada2(n if r >= 2 else n - 1, (r - 2) % 8)
            for r in range(8):
                load_unit(U_GV // 4 + r // 4, r % 4)
                if r < 2:
                    load_ada2(11, 6 + r)
            sp.wait_ge(mod2_made, 12)
            sp.dma_start(ws[:], ws_t).then_inc(ws_landed, 16)
            sp.dma_start(bs[:], bs_row.partition_broadcast(P)).then_inc(ws_landed, 16)
            for t in range(TT):
                sp.dma_start(x_res[:, t], x[t * P:(t + 1) * P, :]).then_inc(x_res_landed, 16)
            with sp.Fori(U_GV // 4 + 2, U_OUT // 4 + 2) as q:
                for r in range(4):
                    load_unit(q, r)
            with sp.Fori(0, 2) as k:
                m = 0
                for u in range(12):
                    load_unit(3 * k + (U_OUT // 4 + 2 + u // 4), u % 4)
                    for _ in range(2 if u % 3 == 2 else 1):
                        load_ada2(2 * k + (12 + m // 8), m % 8, ada_w2)
                        m += 1
            with sp.Fori(U_MLP // 4, U_MLP // 4 + 8) as q:
                for r in range(4):
                    load_unit(q, r)
            sp.wait_ge(mod2_made, 16)
            sp.dma_start(fin_row[:], final_row.partition_broadcast(P)).then_inc(fin_landed, 16)
            with sp.Fori(U_MLP // 4 + 8, UNITS // 4) as q:
                for r in range(4):
                    load_unit(q, r)
            for t in range(TT):
                sp.wait_ge(fin_ready, t + 1)
                sp.dma_start(out[t * P:(t + 1) * P, :], x_res[:, t]).then_inc(stored, 16)
            sp.wait_ge(stored, 16 * TT)

        @block.gpsimd
        def _(pool):
            def lo_unit(q, r):
                pool.wait_ge(hi_done, 4 * q + r + 1)
                pool.tensor_tensor(w_lo[:, r % 2], raw[:, r], w_hi[:, r % 2].bitcast(F32), ALU.subtract).then_inc(lo_done, 1)

            with pool.Fori(0, DVE_CUTS // 4) as q:
                for r in range(4):
                    lo_unit(q, r)
            for r in range(2):
                lo_unit(DVE_CUTS // 4, r)
            pool.wait_ge(lo_done, DVE_CUTS + 4 * HEADS)
            for r in (2, 3):
                lo_unit(DVE_CUTS // 4 + HEADS, r)
            with pool.Fori(DVE_CUTS // 4 + HEADS + 1, UNITS // 4) as q:
                for r in range(4):
                    lo_unit(q, r)

        @block.scalar
        def _(act):
            for dst, src in ((lbl[:].rearrange("p a b -> p (a b)"), small), (ident[:], masks[0])):
                act.dma_start(dst, src).then_inc(small_landed, 16)
            act.dma_start(mask_f32[:], masks[1]).then_inc(small_landed, 16)
            act.wait_ge(cols_landed, 16)
            act.activation(cs[:], C_COL, ACT.Silu).then_inc(cs_ready, 1)
            act.wait_ge(lb_step, 2)
            act.activation(lbt[:, 1:3], lbt[:, 1:3], ACT.Exp).then_inc(lb_exp, 1)

            def hi_unit(q, r, static=False):
                if not (static and q == 0 and r < 2):
                    act.wait_ge(unit_used, 4 * q + r - 1)
                act.wait_ge(raw_landed[r], 16 * q + 16)
                act.activation(w_hi[:, r % 2], raw[:, r], ACT.Copy).then_inc(hi_done, 1)

            def hi_next(u0, q, j):
                hi_unit(q + (u0 // 4 + (j + 2) // 4), (j + 2) % 4)

            def roots(n0, count, width, wait_for=True):
                for t in range(count):
                    act.wait_ge(sumsq, n0 + t + 1)
                act.activation(stat[:, n0:n0 + count], stat[:, n0:n0 + count], ACT.Sqrt, bias=stat[:, 63:64], scale=1.0 / width).then_inc(root, 1)

            def prep(n0, count, ntok, hi, s, b):
                for i in range(count):
                    n = n0 + i
                    kt = n % KT
                    act.wait_ge(turned, n + 1)
                    act.activation(hi[:, kt], bank[4 + n % 4][:, 0:ntok], ACT.Identity, bias=b(kt), scale=s(kt)).then_inc(prep_hi, 1)

            act.wait_ge(ones_ready, 2)
            act.wait_ge(ctx_landed, 16 * CT)
            for t in range(CT):
                if t:
                    act.wait_ge(sumsq, t)
                act.activation(x_tok[:, 0], ctx_tok[:, t], ACT.Square, accum_out=stat[:, t:t + 1]).then_inc(sumsq, 1)
            roots(0, CT, D)
            hi_unit(0, 0, True)
            hi_unit(0, 1, True)
            act.wait_ge(ada1_done, 1)
            for g in range(4):
                act.activation(ada1_row[0:2, g], bank[g][0:2, :], ACT.Copy).then_inc(ada1_rows, 1)
            act.wait_ge(mod1_step, 2)

            def prep_ctx(n0, count):
                prep(n0, count, CTX, c_hi, lambda k: mod1[:, 1, k, 1:2], lambda k: mod1[:, 0, k, 1:2])

            prep_ctx(0, 6)
            for j in range(16):
                hi_next(U_CTX_V, 0, j)
                if j < 5:
                    prep_ctx(6 + 2 * j, 2)
                if j in (2, 3, 4, 5):
                    t = j - 2
                    act.wait_ge(x_landed, 16 * TT)
                    if t:
                        act.wait_ge(sumsq, CT + t)
                    act.activation(junk[:], x_tok[:, t], ACT.Square, accum_out=stat[:, 2 + t:3 + t]).then_inc(sumsq, 1)
                if j == 5:
                    roots(2, TT, D)
                if j >= 8:
                    prep(KT + 2 * (j - 8), 2, SEQ, h_hi, lambda k: mod1[:, 1, k, 0:1], lambda k: mod1[:, 0, k, 0:1])
                if j % 8 == 7:
                    for t in range(CT):
                        act.wait_ge(unit_used, U_CTX_V + j + 1)
                        act.activation(v_ctx[:, t, (j // 8) * 512:(j // 8 + 1) * 512], bank[2 * (j // 8) + t][:], ACT.Copy).then_inc(cv_read, 1)

            def c_ktok_out(h):
                act.wait_ge(c_turned, h + 1)
                act.activation(c_ktok[:], bank[6][:].rearrange("p (a b) -> p a b", b=P), ACT.Copy).then_inc(c_ktok_ready, 1)

            def c_head_act(h, first):
                for j in range(4):
                    hi_next(U_CTX_HEADS, h, j)
                    if j % 2 == 1:
                        d = j // 2
                        act.wait_ge(unit_used, 4 * h + (U_CTX_HEADS + j + 1))
                        if not first:
                            act.wait_ge(c_step, 4 * h)
                        elif d == 0:
                            act.wait_ge(prep_lo, 2 * KT)
                        act.activation(c_sig[:, d], bank[d][:, 0:CTX], ACT.Sigmoid).then_inc(cgate_read, 1)
                    if j == 2 and not first:
                        c_ktok_out(h - 1)

            c_head_act(0, True)
            with act.Fori(1, HEADS) as h:
                c_head_act(h, False)

            def v_out(i):
                act.wait_ge(v_turned, i + 1)
                act.activation(v_lat[:, :, (4 + i) * P:(5 + i) * P], bank[(0, 1, 2, 4)[i]][:].rearrange("p (c v) -> p c v", v=P), ACT.Copy).then_inc(v_read, 1)

            for j in range(16):
                hi_next(U_V, 0, j)
                if j == 0:
                    c_ktok_out(HEADS - 1)
                if j == 7:
                    for t in range(TT):
                        act.wait_ge(unit_used, U_V + j + 1)
                        act.activation(v_lat[:, t, 0:512], bank[t][:], ACT.Copy).then_inc(v_read, 1)
                if j > 8 and j % 2 == 1:
                    i = (j - 9) // 2
                    if i >= 2:
                        act.wait_ge(v_turned, i - 1)
                    act.wait_ge(unit_used, U_V + j + 1)
                    act.activation(v_cols[:, i % 2].rearrange("p (c r) -> p c r", r=ROWS), bank[4 + i][:].rearrange("p (r c) -> p c r", c=GRID_W),
                                   ACT.Copy).then_inc(vt_made, 1)
                if j in (12, 14):
                    v_out((j - 12) // 2)

            def scan_act(h, part):
                if part == 0:
                    act.wait_ge(k_turned, h + 1)
                    for d in range(2):
                        act.activation(ktok[:, 3 * d:3 * d + 3], bank[7 - d][:, 0:384].rearrange("p (a b) -> p a b", b=P), ACT.Copy).then_inc(ktok_ready, 1)
                if part == 1:
                    act.wait_ge(o_done, h + 1)
                    for c in range(TT):
                        act.activation(score[:, c], bank[6][:, c * P:(c + 1) * P], ACT.Square, accum_out=stat[:, 16 + c:17 + c]).then_inc(o_root, 1)
                    act.wait_ge(o_root, 5 * h + TT)
                    act.activation(stat[:, 16:20], stat[:, 16:20], ACT.Sqrt, bias=stat[:, 63:64], scale=1.0 / P).then_inc(o_root, 1)

            def permuted(ap, scanned):
                return ap.rearrange("p (r c) -> p c r", c=GRID_W) if scanned else ap

            def straight(ap, scanned):
                return ap.rearrange("p (c r) -> p c r", r=ROWS) if scanned else ap

            def head_act(h, u0, scanned, first, scan_of):
                for j in range(8):
                    if scan_of is not None and j in (4, 6):
                        scan_act(scan_of, j // 2 - 2)
                    hi_next(u0, 2 * h, j)
                    if first and j in (0, 2):
                        v_out(2 + j // 2)
                    if j == 1:
                        act.wait_ge(unit_used, 8 * h + (u0 + j + 1))
                        if not first:
                            act.wait_ge(scores_done, 8 * (h - 1) + 1)
                        act.activation(straight(q_sb[:], scanned), permuted(bank[0][:], scanned), ACT.Copy).then_inc(proj_read, 1)
                    if j in (3, 5):
                        d = j // 2 - 1
                        act.wait_ge(unit_used, 8 * h + (u0 + j + 1))
                        act.activation(straight(sig[:, d], scanned), permuted(bank[1 + d][:], scanned), ACT.Sigmoid).then_inc(proj_read, 1)
                    if j == 7:
                        act.wait_ge(unit_used, 8 * h + (u0 + j + 1))
                        if not first:
                            act.wait_ge(head_out, h)
                        act.activation(g_sb[:], bank[3][:], ACT.Silu).then_inc(proj_read, 1)

            head_act(0, U_HEADS, False, True, None)
            with act.Fori(1, 4) as h:
                head_act(h, U_HEADS, False, False, h - 1)
            head_act(4, U_HEADS, True, False, 3)
            with act.Fori(5, HEADS) as h:
                head_act(h, U_HEADS, True, False, h - 1)

            for j in range(16):
                if j in (4, 6):
                    scan_act(HEADS - 1, j // 2 - 2)
                hi_next(U_GU, 0, j)
                if j % 2 == 1:
                    act.wait_ge(unit_used, U_GU + j + 1)
                    act.activation(mix[:, j // 2], bank[(j // 2) % 4][:], ACT.Gelu_apprx_tanh).then_inc(u_read, 1)

            def gate_row_out(g, row):
                for c in range(4):
                    act.wait_ge(row_done, 4 * g + c + 1)
                    act.activation(row[:, c * 512:(c + 1) * 512], bank[4 + c][:], ACT.Copy).then_inc(row_read, 1)

            def gv_roots(c):
                act.wait_ge(gv_step, 8 * (c + 1))
                act.activation(stat[:, 20:36], stat[:, 20:36], ACT.Sqrt, bias=stat[:, 63:64], scale=1.0 / P).then_inc(gv_root, 1)

            def gv_out(c, t):
                act.wait_ge(unit_used, U_GV + 8 * c + 8)
                act.activation(gv[:, c, t], bank[4 * c + t][:], ACT.Gelu_apprx_tanh).then_inc(gv_read, 1)

            for j in range(16):
                hi_next(U_GV, 0, j)
                if j == 3:
                    act.wait_ge(head_out, HEADS)
                    gate_row_out(0, g1_row)
                if j == 7:
                    for t in range(TT):
                        gv_out(0, t)
                if j == 9:
                    gv_roots(0)

            def row_squares(c):
                for t in range(TT):
                    act.wait_ge(x_res_ready, 4 * c + t + 1)
                    if c == 0 and t == 0:
                        act.wait_ge(split_lo, 16)
                    act.activation(x_norm[:, t, c * 512:(c + 1) * 512], x_res[:, t, c * 512:(c + 1) * 512], ACT.Square,
                                   accum_out=stat[:, 36 + 4 * t + c:37 + 4 * t + c]).then_inc(part_squared, 1)

            def split(i):
                kt = (i + 8) % KT
                if i == 8:
                    act.wait_ge(mix_a_ready, 4)
                if i == 12:
                    act.wait_ge(mix_a_ready, 8)
                act.activation(h_hi[:, kt], mix[:, kt], ACT.Copy).then_inc(split_hi, 1)

            act.wait_ge(head_out, HEADS)
            act.wait_ge(unit_used, U_OUT)
            for i in range(4):
                split(i)
            for t in range(TT):
                gv_out(1, t)
                if t % 2 == 1:
                    split(3 + t)
                    split(4 + t)
            for j in range(32):
                if j == 0:
                    gv_roots(1)
                hi_next(U_OUT, 0, j)
                if j in (12, 20, 28):
                    row_squares(j // 8 - 1)
                if j in (1, 4):
                    for i in range(4):
                        split(8 + 4 * (j // 4) + i)
            row_squares(3)
            act.wait_ge(total_squared, 1)
            act.activation(stat[:, 6:10], stat[:, 6:10], ACT.Sqrt, bias=stat[:, 63:64], scale=1.0 / D).then_inc(root, 1)
            act.wait_ge(rstd, 3)

            def norm_res(c):
                for t in (2, 3):
                    act.activation(x_norm[:, t, c * 512:(c + 1) * 512], x_res[:, t, c * 512:(c + 1) * 512], ACT.Copy,
                                   scale=stat[:, 6 + t:7 + t]).then_inc(normed_act, 1)

            norm_res(0)
            act.wait_ge(mod2_step, 2)
            for c in range(4):
                if c < 3:
                    norm_res(c + 1)
                for i in range(4 * c, 4 * c + 4):
                    if i == 13:
                        hi_next(U_MLP, 0, 0)
                        hi_next(U_MLP, 0, 1)
                    prep(2 * KT + i, 1, SEQ, h_hi, lambda k: mod2[:, 2, k:k + 1], lambda k: mod2[:, 1, k:k + 1])

            act.wait_ge(prep_lo, 3 * KT)

            def hid_act(b, t):
                first = isinstance(b, int) and b == 0 and t == 0
                act.wait_ge(unit_used, 32 * b + (U_MLP + (3 if first else 2 * t + 2)))
                if not (isinstance(b, int) and b == 0 and t < 2):
                    act.wait_ge(hid_made, HT * b + t - 1)
                act.activation(relu_sb[:, t % 2], bank[t % 4][:], ACT.Relu).then_inc(relu_made, 1)
                act.wait_ge(hid_made, HT * b + t + 1)
                act.activation(hid_hi[:, t], hid_sb[:, t % 2], ACT.Copy).then_inc(hid_hi_made, 1)

            def mlp_act(b):
                for j in range(32):
                    if not (isinstance(b, int) and b == 0 and j < 2):
                        hi_next(U_MLP, 8 * b, j)
                    if isinstance(b, int) and b == 0 and j == 8:
                        gate_row_out(1, g2_row)
                    if isinstance(b, int) and b == 0 and j in (1, 2, 3):
                        if j > 1:
                            hid_act(b, j - 2)
                    elif j < 16 and j % 2 == 1:
                        hid_act(b, j // 2)

            mlp_act(0)
            with act.Fori(1, BLOCKS - 1) as b:
                mlp_act(b)
            for j in range(32):
                if j < 30:
                    hi_next(U_MLP, 8 * (BLOCKS - 1), j)
                if j < 16 and j % 2 == 1:
                    hid_act(BLOCKS - 1, j // 2)
            for t in range(TT):
                act.wait_ge(ff2_added, 16 * (BLOCKS - 1) + 12 + t + 1)
                act.activation(junk[:], x_res[:, t], ACT.Square, accum_out=stat[:, 10 + t:11 + t]).then_inc(sumsq, 1)
                act.wait_ge(sumsq, CT + TT + t + 1)
                act.activation(stat[:, 10 + t:11 + t], stat[:, 10 + t:11 + t], ACT.Sqrt, bias=stat[:, 63:64], scale=1.0 / D).then_inc(root, 1)

        @block.vector
        def _(dve):
            dve.memset(ones[:], 1.0).then_inc(ones_ready, 1)
            dve.memset(stat[:, 63:64], EPS).then_inc(ones_ready, 1)
            dve.memset(c_decay[:], 1.0).then_inc(ones_ready, 1)
            dve.wait_ge(cols_landed, 16)
            dve.wait_ge(small_landed, 48)
            dve.tensor_copy(mask[:], mask_f32[:]).then_inc(mask_ready, 1)
            dve.tensor_tensor(lbt[:, 0], lbl[:, 0], lbl[:, 1], ALU.max).then_inc(lb_ready, 1)
            dve.wait_ge(lb_ready, 1)
            for i in range(2):
                dve.tensor_tensor(lbt[:, 1 + i], lbl[:, i], lbt[:, 0], ALU.subtract).then_inc(lb_step, 1)
            dve.wait_ge(lb_exp, 1)
            dve.tensor_tensor(lbt[:, 0], lbt[:, 1], lbt[:, 2], ALU.add).then_inc(lb_ready, 1)
            dve.wait_ge(lb_ready, 2)
            dve.reciprocal(lbt[:, 0], lbt[:, 0]).then_inc(lb_ready, 1)
            dve.wait_ge(lb_ready, 3)
            dve.tensor_tensor(lb[:].rearrange("p a b -> p (a b)"), lbt[:, 2], lbt[:, 0], ALU.mult).then_inc(lb_ready, 1)
            dve.wait_ge(lb_ready, 4)
            dve.tensor_scalar(oml[:], lb[:], -1.0, 1.0, ALU.mult, ALU.add).then_inc(lb_ready, 1)

            def norm_rows(n_root, n0, count, dst, src, n_normed):
                dve.wait_ge(root, n_root)
                dve.reciprocal(stat[:, n0:n0 + count], stat[:, n0:n0 + count]).then_inc(rstd, 1)
                dve.wait_ge(rstd, n_root)
                for t in range(count):
                    dve.tensor_scalar(dst[:, t], src[:, t], stat[:, n0 + t:n0 + t + 1], None, ALU.mult).then_inc(normed, 1)

            def prep(n0, count, ntok, tmp, hi, lo, s, b):
                for i in range(count):
                    n = n0 + i
                    kt = n % KT
                    dve.wait_ge(prep_hi, n + 1)
                    if n >= 2:
                        dve.wait_ge(prep_lo, n - 1)
                    dve.tensor_scalar(tmp[:, n % 2, 0:ntok], bank[4 + n % 4][:, 0:ntok], s(kt), b(kt), ALU.mult, ALU.add).then_inc(prep_h, 1)
                    dve.wait_ge(prep_h, n + 1)
                    dve.tensor_tensor(lo[:, kt], tmp[:, n % 2, 0:ntok], hi[:, kt].bitcast(F32), ALU.subtract).then_inc(prep_lo, 1)

            dve.wait_ge(cs_ready, 1)
            for k in range(KT):
                dve.wait_ge(ada1_landed[k % 4], 16 * (k // 4) + 16)
                for c in range(2):
                    w = ada1_w[:, k % 4, 7 * 512:]
                    if k == 0:
                        dve.tensor_scalar(ada1_acc[:, c], w, cs[:, k, c:c + 1], None, ALU.mult).then_inc(ada1_summed, 1)
                    else:
                        dve.wait_ge(ada1_summed, 2 * k + c - 1)
                        dve.scalar_tensor_tensor(ada1_acc[:, c], w, cs[:, k, c:c + 1], ada1_acc[:, c], ALU.mult, ALU.add).then_inc(ada1_summed, 1)
                if k == 5:
                    norm_rows(1, 0, CT, ctx_tok, ctx_tok, 0)
            dve.wait_ge(ada1_done, 1)
            for g in range(4, 7):
                dve.tensor_copy(ada1_row[0:2, g], bank[g][0:2, :]).then_inc(ada1_rows, 1)
            dve.wait_ge(ada1_cols, 1)
            dve.tensor_tensor(mod1[:].rearrange("p a k c -> p (a k) c"), bank[7][:, 0:64].rearrange("p (a c) -> p a c", c=2),
                              B1_COL.unsqueeze(2).to_broadcast([P, 32, 2]), ALU.add).then_inc(mod1_ready, 1)
            dve.wait_ge(mod1_ready, 1)
            dve.tensor_scalar(mod1[:, 1], mod1[:, 1], 1.0, None, ALU.add).then_inc(mod1_step, 1)
            dve.wait_ge(mod1_step, 1)
            dve.tensor_tensor(mod1[:, 1], mod1[:, 1], N1_COL.unsqueeze(2).to_broadcast([P, KT, 2]), ALU.mult).then_inc(mod1_step, 1)
            dve.wait_ge(mod1_step, 2)
            prep(0, KT, CTX, prep_tmp, c_hi, c_lo, lambda k: mod1[:, 1, k, 1:2], lambda k: mod1[:, 0, k, 1:2])
            norm_rows(2, 2, TT, x_tok, x_tok, 2)
            prep(KT, KT, SEQ, prep_tmp, h_hi, h_lo, lambda k: mod1[:, 1, k, 0:1], lambda k: mod1[:, 0, k, 0:1])

            dve.wait_ge(prep_lo, 2 * KT)

            def cut(h, i):
                dve.wait_ge(hi_done, 4 * h + (DVE_CUTS + i + 1))
                dve.tensor_tensor(w_lo[:, i % 2], raw[:, (DVE_CUTS + i) % 4], w_hi[:, i % 2].bitcast(F32), ALU.subtract).then_inc(lo_done, 1)

            def c_head_dve(h, first):
                for d in range(2):
                    cut(h, 2 * d)
                    cut(h, 2 * d + 1)
                    dve.wait_ge(cgate_read, 2 * h + d + 1)
                    if not first:
                        dve.wait_ge(c_kd_ready, 2 * h)
                    dve.tensor_scalar(c_f[:, d], c_sig[:, d], oml[:, d, bass.ds(h, 1)], lb[:, d, bass.ds(h, 1)], ALU.mult, ALU.add).then_inc(c_step, 1)
                    dve.wait_ge(c_step, 4 * h + 2 * d + 1)
                    dve.tensor_scalar(c_k[:, d], c_f[:, d], -1.0, 1.0, ALU.mult, ALU.add).then_inc(c_step, 1)
                n = CTX
                dve.tensor_tensor_scan(c_decay[:, 0, n - 2::-1], c_f[:, 0, n - 1:0:-1], c_f[:, 0, 0:n - 1], 1.0, ALU.mult, ALU.bypass).then_inc(c_scan, 1)
                dve.tensor_tensor_scan(c_decay[:, 1, 1:n], c_f[:, 1, 0:n - 1], c_f[:, 0, 0:n - 1], 1.0, ALU.mult, ALU.bypass).then_inc(c_scan, 1)
                if not first:
                    c_state_out(h - 1)
                dve.wait_ge(c_scan, 2 * h + 2)
                dve.wait_ge(c_step, 4 * h + 4)
                for d in range(2):
                    if not first:
                        dve.wait_ge(c_turned, h)
                    dve.tensor_tensor(c_kd[:, d], c_k[:, d], c_decay[:, d], ALU.mult).then_inc(c_kd_ready, 1)

            def c_state_out(h):
                dve.wait_ge(c_state_done, h + 1)
                dve.tensor_copy(s_ctx[:, bass.ds(h, 1)].rearrange("p a d v -> p (a d v)"), bank[7][:, 0:256]).then_inc(s_ctx_ready, 1)

            dve.wait_ge(ones_ready, 3)
            dve.wait_ge(mask_ready, 1)
            dve.wait_ge(lb_ready, 5)
            dve.wait_ge(lo_done, DVE_CUTS)
            c_head_dve(0, True)
            with dve.Fori(1, HEADS) as h:
                c_head_dve(h, False)
            c_state_out(HEADS - 1)

            def ada2_part(n, m, w=ada_w, acc=ada_acc):
                dve.wait_ge(ada_landed[m % 2], 64 * n + 16 * (m // 2) + 16)
                for t in range(2):
                    i = 2 * m + t
                    c = cs[:, i, 0:1]
                    if i == 0:
                        dve.tensor_scalar(acc[:], w[:, 0, 0], c, None, ALU.mult).then_inc(ada_summed, 1)
                    else:
                        dve.wait_ge(ada_summed, 16 * n + i)
                        dve.scalar_tensor_tensor(acc[:], w[:, m % 2, t], c, acc[:], ALU.mult, ALU.add).then_inc(ada_summed, 1)

            mod2_flat = mod2[:].rearrange("p g k -> p (g k)")

            def ada2_take(n, b=7):
                dve.wait_ge(ada_colsum, n + 1)
                dve.tensor_tensor(mod2_flat[:, bass.ds(4 * n, 4)], bank[b][:, 508:512], B2_COL[:, bass.ds(4 * n, 4)], ALU.add).then_inc(mod2_made, 1)

            dve.wait_ge(c_kd_ready, 2 * HEADS)
            for n in range(3):
                if n:
                    ada2_take(n - 1, 3)
                for m in range(8):
                    ada2_part(n, m)

            off = [0]
            for lv in range(LEVELS + 1):
                off.append(off[-1] + (SEQ >> lv))

            def totals(lv):
                return tot[:, :, off[lv]:off[lv + 1]]

            def gates(h):
                dve.wait_ge(proj_read, 4 * h + 3)
                for d in range(2):
                    dve.tensor_scalar(tot[:, d, 0:SEQ], sig[:, d], oml[:, d, bass.ds(h, 1)], lb[:, d, bass.ds(h, 1)], ALU.mult, ALU.add).then_inc(gate_step, 1)
                dve.wait_ge(gate_step, 6 * h + 2)
                k = (yy[:, 0], xx[:, 1])
                q = (xx[:, 0], yy[:, 1])
                for d in range(2):
                    dve.tensor_scalar(k[d], tot[:, d, 0:SEQ], -1.0, 1.0, ALU.mult, ALU.add).then_inc(gate_step, 1)
                for d in range(2):
                    dve.tensor_tensor(q[d], q_sb[:], tot[:, d, 0:SEQ], ALU.mult).then_inc(gate_step, 1)
                dve.wait_ge(gate_step, 6 * h + 6)
                dve.tensor_tensor(ksum[:], k[0], k[1], ALU.add).then_inc(scan_ready, 1)
                meet(1)

            def meet(L):
                for dst, first, step in ((k_meet, 0, 3), (q_meet, 1, 1)):
                    dims = [[4 * SEQ, P], [2 * L, SEQ // (2 * L)], [step * SEQ + L, 2]] + ([[1, L]] if L > 1 else [])
                    src = bass.AP(kq, first * SEQ, dims)
                    if L == 1:
                        dst = dst[:].rearrange("p (b two) -> p b two", two=2)
                    else:
                        dst = dst[:].rearrange("p (b two l) -> p b two l", two=2, l=L)
                    ins = dve.tensor_copy(dst, src)
                ins.then_inc(level_ready, 1)

            def merge(h, i):
                b = bank[4 + i % 2][:].rearrange("p (c t) -> p c t", t=P)
                if i == 0:
                    dve.wait_ge(scores_done, 8 * h + 1)
                    dve.tensor_copy(score[:], b).then_inc(scores_merged, 1)
                else:
                    dve.copy_predicated(score[:], mask[:, i - 1].unsqueeze(1).to_broadcast([P, TT, P]), b).then_inc(scores_merged, 1)

            def grow(h, i):
                L = 1 << (i - 1)
                dve.wait_ge(level_ready, 7 * h + i)
                if i > 1:
                    dve.wait_ge(tot_ready, 7 * h + i - 1)
                    dve.wait_ge(decayed, 7 * h + i - 1)
                if i == LEVELS:
                    dve.wait_ge(scores_done, 8 * h + i + 1)
                    dve.wait_ge(scores_merged, 8 * h + i)
                t = totals(i - 1).rearrange("p d (b two) -> p d b two", two=2)
                dve.tensor_tensor(totals(i), t[:, :, :, 0], t[:, :, :, 1], ALU.mult).then_inc(tot_ready, 1)
                for a, half in ((xx, 1), (yy, 0)):
                    a = a.rearrange("p d (b two l) -> p d b two l", two=2, l=L)
                    f = t[:, :, :, 1 - half]
                    if L == 1:
                        ins = dve.tensor_tensor(a[:, :, :, half, 0], a[:, :, :, half, 0], f, ALU.mult)
                    else:
                        ins = dve.tensor_tensor(a[:, :, :, half], a[:, :, :, half], f.unsqueeze(3).to_broadcast([P, 2, SEQ // (2 * L), L]), ALU.mult)
                ins.then_inc(decayed, 1)
                if i < LEVELS:
                    dve.wait_ge(scores_done, 8 * h + i + 1)
                    dve.wait_ge(scores_merged, 8 * h + i)
                    dve.wait_ge(decayed, 7 * h + i)
                    meet(2 * L)

            def states(h):
                dve.wait_ge(kv_done, h + 1)
                dve.wait_ge(tot_ready, 7 * h + 7)
                for i in range(3):
                    for d in range(2):
                        c = i if d == 0 else 3 - i
                        before = s_ctx[:, bass.ds(h, 1), d].rearrange("p a v -> p (a v)") if i == 0 else state[:, d, i - 1]
                        if i:
                            dve.wait_ge(states_ready, 6 * h + 2 * (i - 1) + d + 1)
                        slot = c if d == 0 else c - 1
                        dve.scalar_tensor_tensor(state[:, d, i], before, tot[:, d, off[7] + c:off[7] + c + 1],
                                                 bank[7 - d][:, slot * P:(slot + 1) * P], ALU.mult, ALU.add).then_inc(states_ready, 1)

            def o_rows(h):
                dve.wait_ge(o_root, 5 * h + 5)
                dve.reciprocal(stat[:, 16:20], stat[:, 16:20]).then_inc(o_rstd, 1)
                dve.wait_ge(o_rstd, h + 1)
                dve.tensor_tensor(o_norm[:], bank[6][:].rearrange("p (c v) -> p c v", v=P),
                                  stat[:, 16:20].unsqueeze(2).to_broadcast([P, TT, P]), ALU.mult).then_inc(o_ready, 1)

            def head_result(h, scanned):
                dve.wait_ge(o_turned, h + 1)
                dve.wait_ge(proj_read, 4 * h + 4)
                dst = mix[:, bass.ds(h + 8, 1)].rearrange("p a t -> p (a t)")
                src, g = bank[7][:], g_sb[:]
                if scanned:
                    dst, g = (a.rearrange("p (r c) -> p c r", c=GRID_W) for a in (dst, g))
                    src = src.rearrange("p (c r) -> p c r", r=ROWS)
                dve.scalar_tensor_tensor(dst, src, OG_COL[:, bass.ds(h, 1)], g, ALU.mult, ALU.mult).then_inc(head_out, 1)

            def scan_dve(h, scanned, n, then_gates):
                merge(h, 0)
                m = 0
                for i in range(1, LEVELS + 1):
                    grow(h, i)
                    merge(h, i)
                    if i == 3:
                        ada2_take(n - 1)
                    for _ in range((0, 0, 0, 0, 1, 1, 1, 2)[i]):
                        ada2_part(n, m)
                        m += 1
                ada2_part(n, 5)
                states(h)
                if then_gates is not None:
                    dve.wait_ge(o_done, h + 1)
                    gates(then_gates)
                o_rows(h)
                ada2_part(n, 6)
                ada2_part(n, 7)
                head_result(h, scanned)

            gates(0)
            with dve.Fori(1, 5) as h:
                scan_dve(h - 1, False, h + 2, h)
            with dve.Fori(5, HEADS) as h:
                scan_dve(h - 1, True, h + 2, h)
            scan_dve(HEADS - 1, True, 10, None)
            ada2_take(10)
            for m in range(8):
                ada2_part(11, m)
            ada2_take(11)
            dve.wait_ge(mod2_made, 12)
            dve.tensor_scalar(mod2[:, 2], mod2[:, 2], 1.0, None, ALU.add).then_inc(mod2_step, 1)
            dve.wait_ge(mod2_step, 1)
            dve.tensor_tensor(mod2[:, 2], mod2[:, 2], N2_COL, ALU.mult).then_inc(mod2_step, 1)

            rs = stat[:, 20:36].rearrange("p (t h) -> p t h", h=4)

            def gv_squares(c, t0=0, t1=TT):
                for t in range(t0, t1):
                    n = 8 * c + 2 * t
                    dve.wait_ge(gv_read, 4 * c + t + 1)
                    if n:
                        dve.wait_ge(gv_step, n)
                    dve.tensor_tensor(g_tmp[:, t % 2], gv[:, c, t], gv[:, c, t], ALU.mult).then_inc(gv_step, 1)
                    dve.wait_ge(gv_step, n + 1)
                    dve.tensor_reduce(rs[:, t], g_tmp[:, t % 2].rearrange("p (h d) -> p h d", d=P), AX.X, ALU.add).then_inc(gv_step, 1)

            def gv_norm(c):
                dve.wait_ge(gv_root, c + 1)
                dve.reciprocal(stat[:, 20:36], stat[:, 20:36]).then_inc(gv_rstd, 1)
                dve.wait_ge(gv_rstd, c + 1)
                for t in range(TT):
                    v = gv[:, c, t].rearrange("p (h d) -> p h d", d=P)
                    dve.tensor_tensor(v, v, rs[:, t].unsqueeze(2).to_broadcast([P, 4, P]), ALU.mult).then_inc(gv_ready, 1)

            def mixing(c):
                for i in range(4):
                    h = 4 * c + i
                    dve.wait_ge(mixed_head, h + 1)
                    if i == 0:
                        dve.wait_ge(gv_ready, 4 * c + 4)
                    if h >= 2:
                        dve.wait_ge(mix_a_ready, h - 1)
                    dve.scalar_tensor_tensor(g_tmp[:, i % 2].rearrange("p (n t) -> p n t", t=P), bank[4 * c + i][:].rearrange("p (n t) -> p n t", t=P),
                                             VG_COL[:, h:h + 1], bs[:, h].unsqueeze(1).to_broadcast([P, TT, P]), ALU.mult, ALU.add).then_inc(mixed_step, 1)
                    dve.wait_ge(mixed_step, h + 1)
                    dve.tensor_tensor(mix[:, h], mix[:, h], g_tmp[:, i % 2], ALU.mult).then_inc(mix_a_ready, 1)

            dve.wait_ge(u_read, 8)
            gv_squares(0)
            gv_norm(0)
            dve.wait_ge(ws_landed, 32)
            mixing(0)

            def split(i):
                kt = (i + 8) % KT
                dve.wait_ge(split_hi, i + 1)
                dve.tensor_tensor(h_lo[:, kt], mix[:, kt], h_hi[:, kt].bitcast(F32), ALU.subtract).then_inc(split_lo, 1)

            for i in range(4):
                split(i)
            for t in (0, 2):
                gv_squares(1, t, t + 2)
                split(4 + t)
                split(5 + t)
            gv_norm(1)
            for i in range(8, 12):
                split(i)
            mixing(1)
            for i in range(12, 16):
                split(i)

            dve.wait_ge(x_res_landed, 16 * TT)
            dve.wait_ge(row_read, 4)

            def first_residual(c):
                for t in range(TT):
                    n = 4 * c + t
                    dve.wait_ge(out_done, 3 * c + t + 1) if t < 3 else dve.wait_ge(unit_used, U_OUT + 8 * (c + 1))
                    if n >= 2:
                        dve.wait_ge(x_res_ready, n - 1)
                    dve.tensor_tensor(g_tmp[:, n % 2], bank[4 * (c % 2) + t][:], g1_row[:, c * 512:(c + 1) * 512], ALU.mult).then_inc(out_tmp, 1)
                    dve.wait_ge(out_tmp, n + 1)
                    dve.tensor_tensor(x_res[:, t, c * 512:(c + 1) * 512], x_res[:, t, c * 512:(c + 1) * 512], g_tmp[:, n % 2], ALU.add).then_inc(x_res_ready, 1)

            def ada2_late(n, m0, m1):
                for m in range(m0, m1):
                    ada2_part(n, m, ada_w2, ada_acc2)

            first_residual(0)
            ada2_late(12, 0, 8)
            ada2_take(12, 3)
            ada2_late(13, 0, 5)
            first_residual(1)
            ada2_late(13, 5, 8)
            ada2_take(13, 7)
            ada2_late(14, 0, 8)
            first_residual(2)
            ada2_take(14, 3)
            ada2_late(15, 0, 8)
            ada2_take(15, 3)
            first_residual(3)
            dve.wait_ge(part_squared, 16)
            dve.tensor_reduce(stat[:, 6:10], stat[:, 36:52].rearrange("p (t c) -> p t c", c=4), AX.X, ALU.add).then_inc(total_squared, 1)
            dve.wait_ge(root, 3)
            dve.reciprocal(stat[:, 6:10], stat[:, 6:10]).then_inc(rstd, 1)
            dve.wait_ge(rstd, 3)

            def norm_res(c):
                for t in (0, 1):
                    dve.tensor_scalar(x_norm[:, t, c * 512:(c + 1) * 512], x_res[:, t, c * 512:(c + 1) * 512], stat[:, 6 + t:7 + t], None,
                                      ALU.mult).then_inc(normed, 1)

            norm_res(0)
            dve.wait_ge(mod2_step, 2)
            for c in range(4):
                if c < 3:
                    norm_res(c + 1)
                prep(2 * KT + 4 * c, 4, SEQ, prep_tmp2, h_hi, h_lo, lambda k: mod2[:, 2, k:k + 1], lambda k: mod2[:, 1, k:k + 1])

            dve.wait_ge(prep_lo, 3 * KT)

            def hid(b, t):
                dve.wait_ge(relu_made, HT * b + t + 1)
                if not (isinstance(b, int) and b == 0 and t < 2):
                    dve.wait_ge(hid_ready, HT * b + t - 1)
                dve.tensor_tensor(hid_sb[:, t % 2], relu_sb[:, t % 2], relu_sb[:, t % 2], ALU.mult).then_inc(hid_made, 1)
                dve.wait_ge(hid_hi_made, HT * b + t + 1)
                dve.tensor_tensor(hid_lo[:, t], hid_sb[:, t % 2], hid_hi[:, t].bitcast(F32), ALU.subtract).then_inc(hid_ready, 1)

            def second_residual(b, c, t):
                n = 4 * c + t
                dve.wait_ge(ff2_done, 12 * b + (3 * c + t + 1)) if t < 3 else dve.wait_ge(unit_used, 32 * b + (U_MLP + 16 + 4 * (c + 1)))
                if not (isinstance(b, int) and b == 0 and n < 2):
                    dve.wait_ge(ff2_added, 16 * b + n - 1)
                dve.tensor_tensor(g_tmp[:, n % 2], bank[4 * (1 - c % 2) + t][:], g2_row[:, c * 512:(c + 1) * 512], ALU.mult).then_inc(ff2_tmp, 1)
                dve.wait_ge(ff2_tmp, 16 * b + n + 1)
                dve.tensor_tensor(x_res[:, t, c * 512:(c + 1) * 512], x_res[:, t, c * 512:(c + 1) * 512], g_tmp[:, n % 2], ALU.add).then_inc(ff2_added, 1)

            def mlp_dve(b):
                for t in range(HT):
                    hid(b, t)
                if isinstance(b, int) and b == 0:
                    dve.wait_ge(row_read, 8)
                for c in range(4):
                    for t in range(TT):
                        second_residual(b, c, t)

            mlp_dve(0)
            with dve.Fori(1, BLOCKS) as b:
                mlp_dve(b)
            dve.wait_ge(fin_landed, 16)
            for t in range(TT):
                dve.wait_ge(root, 4 + t)
                dve.reciprocal(stat[:, 10 + t:11 + t], stat[:, 10 + t:11 + t]).then_inc(rstd, 1)
                dve.wait_ge(rstd, 4 + t)
                dve.scalar_tensor_tensor(x_res[:, t], x_res[:, t], stat[:, 10 + t:11 + t], fin_row[:], ALU.mult, ALU.mult).then_inc(fin_ready, 1)

        @block.tensor
        def _(pe):
            pe.wait_ge(cs_ready, 1)

            for k in range(KT):
                pe.wait_ge(ada1_landed[k % 4], 16 * (k // 4) + 16)
                for g in range(7):
                    mm = pe.matmul(bank[g][0:2, :], cs[:, k], ada1_w[:, k % 4, g * 512:(g + 1) * 512], start=(k == 0), stop=(k == KT - 1))
                mm.then_inc(ada1_used if k < KT - 1 else ada1_done, 1)
            pe.wait_ge(ada1_summed, 2 * KT)
            for j in range(8):
                c, i = j % 2, j // 2
                pe.matmul(bank[7][:, 56 + j:57 + j], ada1_acc[:, c, i * P:(i + 1) * P], ones[:, 0:1], start=True, stop=True)
            pe.wait_ge(ada1_rows, 7)
            for j in range(28):
                mm = pe.transpose(bank[7][:, 2 * j:2 * j + 2], ada1_row[0:2, j // 4, (j % 4) * P:(j % 4 + 1) * P], ident[0:2, 0:2])
            mm.then_inc(ada1_cols, 1)

            def prep(n0, count, src, ntile, n_normed):
                for i in range(count):
                    n = n0 + i
                    kt = n % KT
                    if n < 2 * KT:
                        if kt == 0:
                            pe.wait_ge(normed, n_normed)
                    elif kt % 4 == 0:
                        pe.wait_ge(normed, n_normed + 2 * (kt // 4) + 2)
                        pe.wait_ge(normed_act, 2 * (kt // 4) + 2)
                    if n >= 4:
                        pe.wait_ge(prep_h, n - 3)
                    for t in range(ntile):
                        mm = pe.transpose(bank[4 + n % 4][:, t * P:(t + 1) * P], src[:, t, kt * P:(kt + 1) * P], ident[:])
                    mm.then_inc(turned, 1)

            pe.wait_ge(mod1_ready, 1)
            prep(0, 6, ctx_tok, CT, CT)

            def tall(r, half, dst, hi, lo, between=(None, None)):
                for k in range(8):
                    if k % 4 == 0 and between[k // 4] is not None:
                        between[k // 4]()
                    kt = 8 * half + k
                    wh, wl = w_hi[:, r % 2, k * P:(k + 1) * P], w_lo[:, r % 2, k * P:(k + 1) * P]
                    pe.matmul(dst, wh, hi[:, kt], start=(kt == 0), stop=False)
                    pe.matmul(dst, wh, lo[:, kt], start=False, stop=False)
                    mm = pe.matmul(dst, wl, hi[:, kt], start=False, stop=(kt == KT - 1))
                return mm

            def wide(r, kts, first, last, banks, hi, lo, tokens, wait_tile=None):
                mms = []
                for k in range(2):
                    if wait_tile is not None:
                        wait_tile(k)
                    for t, b in enumerate(banks):
                        xh, xl = tokens(hi, kts[k], t), tokens(lo, kts[k], t)
                        wh, wl = w_hi[:, r % 2, k * 512:(k + 1) * 512], w_lo[:, r % 2, k * 512:(k + 1) * 512]
                        pe.matmul(b[:], xh, wh, start=(first and k == 0), stop=False)
                        pe.matmul(b[:], xh, wl, start=False, stop=False)
                        mm = pe.matmul(b[:], xl, wh, start=False, stop=(last and k == 1))
                        if last and k == 1:
                            mms.append(mm)
                return mm, mms

            def raster(a, kt, t):
                return a[:, kt, t * P:(t + 1) * P]

            for j in range(16):
                pe.wait_ge(lo_done, U_CTX_V + j + 1)
                c, i = j // 8, j % 8
                if c == 0:
                    pe.wait_ge(prep_lo, 2 * i + 2)
                mm, _ = wide(j % 4, (2 * i, 2 * i + 1), i == 0, i == 7, bank[2 * c:2 * c + 2], c_hi, c_lo, raster)
                mm.then_inc(unit_used, 1)
                if j < 5:
                    prep(6 + 2 * j, 2, ctx_tok, CT, CT)
                if j >= 8:
                    prep(KT + 2 * (j - 8), 2, x_tok, TT, CT + TT)

            def c_turn(h):
                pe.wait_ge(c_kd_ready, 2 * h + 2)
                for d in range(2):
                    for t in range(CT):
                        mm = pe.transpose(bank[6][:, (2 * d + t) * P:(2 * d + t + 1) * P], c_kd[:, d, t * P:(t + 1) * P], ident[:])
                mm.then_inc(c_turned, 1)

            def c_states(h):
                pe.wait_ge(c_ktok_ready, h + 1)
                for d in range(2):
                    for t in range(CT):
                        mm = pe.matmul(bank[7][:, d * P:(d + 1) * P], c_ktok[:, 2 * d + t], v_ctx[:, t, bass.ds(P * h, P)], start=(t == 0), stop=(t == CT - 1))
                mm.then_inc(c_state_done, 1)

            def c_head_pe(h, first):
                for j in range(4):
                    pe.wait_ge(lo_done, 4 * h + (U_CTX_HEADS + j + 1))
                    d = j // 2
                    if j % 2 == 0 and not first:
                        pe.wait_ge(cgate_read, 2 * h - 1 + d)
                    if j == 2 and not first:
                        c_turn(h - 1)
                    tall(j, j % 2, bank[d][:, 0:CTX], c_hi, c_lo).then_inc(unit_used, 1)
                if not first:
                    c_states(h - 1)

            pe.wait_ge(cv_read, 2)
            c_head_pe(0, True)
            with pe.Fori(1, HEADS) as h:
                c_head_pe(h, False)

            def ada2_colsum(n, b=7, acc=ada_acc):
                pe.wait_ge(ada_summed, 16 * n + 16)
                for i in range(4):
                    mm = pe.matmul(bank[b][:, 508 + i:509 + i], acc[:, i * P:(i + 1) * P], ones[:, 0:1], start=True, stop=True)
                mm.then_inc(ada_colsum, 1)

            V_BANK = (0, 1, 2, 4)

            def v_turn_pe(i):
                pe.wait_ge(vt_made, i + 1)
                pe.wait_ge(v_read, 4)
                for c in range(TT):
                    mm = pe.transpose(bank[V_BANK[i]][:, c * P:(c + 1) * P], v_cols[:, i % 2, c * P:(c + 1) * P], ident[:])
                mm.then_inc(v_turned, 1)

            for j in range(16):
                pe.wait_ge(lo_done, U_V + j + 1)
                c, i = j // 8, j % 8
                if i == 0 and c == 0:
                    pe.wait_ge(cgate_read, 2 * HEADS)
                if j == 8:
                    pe.wait_ge(s_ctx_ready, HEADS)
                if c == 0:
                    mm, _ = wide(j % 4, (2 * i, 2 * i + 1), i == 0, i == 7, bank[0:4], h_hi, h_lo, raster)
                else:
                    mm = tall(j % 4, j % 2, bank[4 + i // 2][:], h_hi, h_lo)
                mm.then_inc(unit_used, 1)
                if j in (11, 13, 15):
                    v_turn_pe((j - 11) // 2)
                if j == 1:
                    c_turn(HEADS - 1)
                if j == 3:
                    c_states(HEADS - 1)
                if j == 8:
                    pe.wait_ge(v_read, 4)
                    ada2_colsum(0, 3)

            def step(h, i):
                if i <= LEVELS:
                    b = bank[4 + i % 2]
                    if i == 0:
                        pe.wait_ge(scan_ready, h + 1)
                    if i >= 2:
                        pe.wait_ge(scores_merged, 8 * h + i - 1)
                    if i >= 1:
                        pe.wait_ge(level_ready, 7 * h + i)
                    k, q = (ksum, q_sb) if i == 0 else (k_meet, q_meet)
                    for c in range(TT):
                        whole = slice(c * P, (c + 1) * P)
                        mm = pe.matmul(b[:, whole], k[:, whole], q[:, whole], start=True, stop=True)
                    mm.then_inc(scores_done, 1)
                elif i == 8:
                    pe.wait_ge(mod2_made, h + 3)
                    pe.wait_ge(decayed, 7 * h + 7)
                    for c in range(3):
                        pe.transpose(bank[7][:, c * P:(c + 1) * P], yy[:, 0, c * P:(c + 1) * P], ident[:])
                        mm = pe.transpose(bank[6][:, c * P:(c + 1) * P], xx[:, 1, (c + 1) * P:(c + 2) * P], ident[:])
                    mm.then_inc(k_turned, 1)
                elif i == 9:
                    pe.wait_ge(ktok_ready, 2 * h + 2)
                    for c in range(3):
                        pe.matmul(bank[7][:, c * P:(c + 1) * P], ktok[:, c], v_lat[:, c, bass.ds(P * h, P)], start=True, stop=True)
                        mm = pe.matmul(bank[6][:, c * P:(c + 1) * P], ktok[:, 3 + c], v_lat[:, c + 1, bass.ds(P * h, P)], start=True, stop=True)
                    mm.then_inc(kv_done, 1)
                elif i == 10:
                    pe.wait_ge(states_ready, 6 * h + 6)
                    pe.wait_ge(scores_merged, 8 * h + 8)
                    for c in range(TT):
                        whole = slice(c * P, (c + 1) * P)
                        ctx_state = lambda d: s_ctx[:, bass.ds(h, 1), d].rearrange("p a v -> p (a v)")
                        sf = ctx_state(0) if c == 0 else state[:, 0, c - 1]
                        sb = ctx_state(1) if c == 3 else state[:, 1, 2 - c]
                        pe.matmul(bank[6][:, whole], score[:, c], v_lat[:, c, bass.ds(P * h, P)], start=True, stop=False)
                        pe.matmul(bank[6][:, whole], xx[:, 0, whole], sf, start=False, stop=False)
                        mm = pe.matmul(bank[6][:, whole], yy[:, 1, whole], sb, start=False, stop=True)
                    mm.then_inc(o_done, 1)
                else:
                    pe.wait_ge(o_ready, h + 1)
                    for c in range(TT):
                        mm = pe.transpose(bank[7][:, c * P:(c + 1) * P], o_norm[:, c], ident[:])
                    mm.then_inc(o_turned, 1)

            def steps(h, slot):
                if h is None or slot not in STEP_SLOTS:
                    return None

                def run():
                    for i in STEP_SLOTS[slot]:
                        step(h, i)
                return run

            def head_pe(h, first, scan_of):
                for j in range(8):
                    pe.wait_ge(lo_done, 8 * h + (U_HEADS + j + 1))
                    b = j // 2
                    if j % 2 == 0 and not first:
                        pe.wait_ge(proj_read, 4 * (h - 1) + b + 1)
                    if first and j in (0, 2, 4):
                        pe.wait_ge(v_read, 5 + b)
                    if first and j == 6:
                        pe.wait_ge(mod2_made, 2)
                    mm = tall(j % 4, j % 2, bank[b][:], h_hi, h_lo, (steps(scan_of, 2 * j), steps(scan_of, 2 * j + 1)))
                    mm.then_inc(unit_used, 1)
                    if first and j == 1:
                        v_turn_pe(3)
                    if j == 0:
                        if first:
                            pe.wait_ge(mod2_made, 1)
                            ada2_colsum(1, 3)
                        else:
                            ada2_colsum(h + 1)

            head_pe(0, True, None)
            with pe.Fori(1, HEADS) as h:
                head_pe(h, False, h - 1)

            for j in range(16):
                pe.wait_ge(lo_done, U_GU + j + 1)
                b = j // 2
                if j % 2 == 0:
                    if b < 4:
                        pe.wait_ge(proj_read, 4 * (HEADS - 1) + b + 1)
                    else:
                        pe.wait_ge(u_read, b - 3)
                last_scan = HEADS - 1 if j < 8 else None
                mm = tall(j % 4, j % 2, bank[b % 4][:], h_hi, h_lo, (steps(last_scan, 2 * j), steps(last_scan, 2 * j + 1)))
                mm.then_inc(unit_used, 1)
                if j == 0:
                    ada2_colsum(9)
                if j == 8:
                    pe.wait_ge(head_out, HEADS)
                    ada2_colsum(10)

            def gate_row(g):
                for c in range(4):
                    for i in range(4):
                        k = 4 * c + i
                        src = mod2[:, 3 * g, k:k + 1].to_broadcast([P, P])
                        mm = pe.matmul(bank[4 + c][:, i * P:(i + 1) * P], src, ident[:], start=True, stop=True)
                    mm.then_inc(row_done, 1)

            def mix_heads(c):
                pe.wait_ge(ws_landed, 32)
                pe.wait_ge(gv_ready, 4 * c + 4)
                for i in range(4):
                    for n in range(TT):
                        mm = pe.matmul(bank[4 * c + i][:, n * P:(n + 1) * P], gv[:, c, n, i * P:(i + 1) * P], ws[:, 4 * c + i], start=True, stop=True)
                    mm.then_inc(mixed_head, 1)

            for j in range(16):
                pe.wait_ge(lo_done, U_GV + j + 1)
                c, i = j // 8, j % 8
                if j == 0:
                    pe.wait_ge(u_read, 8)
                if j == 8:
                    pe.wait_ge(row_read, 4)
                mm, _ = wide(j % 4, (2 * i, 2 * i + 1), i == 0, i == 7, bank[4 * c:4 * c + 4], h_hi, h_lo, raster)
                mm.then_inc(unit_used, 1)
                if j == 0:
                    pe.wait_ge(mod2_made, 11)
                    ada2_colsum(11)
                if j == 2:
                    pe.wait_ge(mod2_made, 12)
                    gate_row(0)
                if j == 11:
                    mix_heads(0)

            for j in range(32):
                pe.wait_ge(lo_done, U_OUT + j + 1)
                c, i = j // 8, j % 8
                if i == 0:
                    if c == 0:
                        pe.wait_ge(mixed_step, 4)
                    elif c == 1:
                        pe.wait_ge(mixed_step, 8)
                    else:
                        pe.wait_ge(out_tmp, 4 * (c - 1))
                        pe.wait_ge(mod2_made, 11 + c)
                if j == 4:
                    pe.wait_ge(gv_read, 8)
                    mix_heads(1)
                order = [(2 * i + k + 8) % KT for k in range(2)]
                tile_ready = (lambda k, i=i: pe.wait_ge(split_lo, 2 * i + k + 1)) if c == 0 else None
                mm, mms = wide(j % 4, order, i == 0, i == 7, bank[4 * (c % 2):4 * (c % 2) + 4], h_hi, h_lo, raster, tile_ready)
                for m in mms[:-1]:
                    m.then_inc(out_done, 1)
                mm.then_inc(unit_used, 1)
                if j in (12, 18, 25, 30):
                    n = 10 + j // 6
                    pe.wait_ge(out_tmp, 4 * (n - 11) if n < 15 else 12)
                    if n == 15:
                        pe.wait_ge(mod2_made, 15)
                    ada2_colsum(n, 7 if n == 13 else 3, ada_acc2)

            pe.wait_ge(out_tmp, 16)
            prep(2 * KT, 5, x_norm, TT, CT + TT)

            def first_units():
                for half in range(2):
                    for k in range(8):
                        kt = 8 * half + k
                        for t in range(2):
                            if k == 0:
                                pe.wait_ge(lo_done, U_MLP + 2 * half + t + 1)
                            if t == 0:
                                pe.wait_ge(prep_lo, 2 * KT + kt + 1)
                            wh, wl = w_hi[:, t, k * P:(k + 1) * P], w_lo[:, t, k * P:(k + 1) * P]
                            pe.matmul(bank[t][:], wh, h_hi[:, kt], start=(kt == 0), stop=False)
                            pe.matmul(bank[t][:], wh, h_lo[:, kt], start=False, stop=False)
                            mm = pe.matmul(bank[t][:], wl, h_hi[:, kt], start=False, stop=(kt == KT - 1))
                            if k == 7:
                                mm.then_inc(unit_used, 1)
                        if kt < 8:
                            prep(2 * KT + kt + 5, 1, x_norm, TT, CT + TT)
                    if half == 0:
                        prep(3 * KT - 3, 3, x_norm, TT, CT + TT)

            def mlp_pe(b, first):
                if first:
                    first_units()
                for j in range(4 if first else 0, 16):
                    pe.wait_ge(lo_done, 32 * b + (U_MLP + j + 1))
                    t = j // 2
                    if j % 2 == 0:
                        if t < 4:
                            if not first:
                                pe.wait_ge(ff2_tmp, 16 * (b - 1) + 12 + t + 1)
                        else:
                            pe.wait_ge(relu_made, HT * b + t - 3)
                    tall(j % 4, j % 2, bank[t % 4][:], h_hi, h_lo).then_inc(unit_used, 1)
                    if first and j == 5:
                        pe.wait_ge(mod2_made, 16)
                        gate_row(1)
                for j in range(16):
                    pe.wait_ge(lo_done, 32 * b + (U_MLP + 16 + j + 1))
                    c, i = j // 4, j % 4
                    banks = bank[4:8] if c % 2 == 0 else bank[0:4]
                    if i == 0:
                        if c == 0:
                            if first:
                                pe.wait_ge(row_read, 8)
                            else:
                                pe.wait_ge(ff2_tmp, 16 * (b - 1) + 12)
                        elif c == 1:
                            pe.wait_ge(relu_made, HT * b + HT)
                        else:
                            pe.wait_ge(ff2_tmp, 16 * b + 4 * (c - 1))
                    tile_ready = (lambda k, i=i: pe.wait_ge(hid_ready, HT * b + 2 * i + k + 1)) if c == 0 else None
                    mm, mms = wide(j % 4, (2 * i, 2 * i + 1), i == 0, i == 3, banks, hid_hi, hid_lo, raster, tile_ready)
                    for m in mms[:-1]:
                        m.then_inc(ff2_done, 1)
                    mm.then_inc(unit_used, 1)

            mlp_pe(0, True)
            with pe.Fori(1, BLOCKS) as b:
                mlp_pe(b, False)


def tall_units(w):
    n = w.shape[1] // P
    return w.reshape(2, 8, P, n, P).transpose(3, 0, 2, 1, 4).reshape(2 * n, P, UNIT)


def wide_units(w):
    k, n = w.shape[0] // (2 * P), w.shape[1] // 512
    return w.reshape(k, 2, P, n, 512).transpose(3, 0, 2, 1, 4).reshape(n * k, P, UNIT)


def kernel(**inputs):
    import numpy as np
    import concourse.bacc as bacc
    from concourse.bass_utils import run_bass_kernel_spmd as run

    a = {k: np.asarray(v) for k, v in inputs.items()}
    w_in, w_out, w1, w2 = a["w_in"][0], a["w_out"][0], a["w_ff1"][0], a["w_ff2"][0]
    U, V, Q, I, FF, FB, G = (w_in[:, 1024 * i:1024 * (i + 1)] for i in range(7))

    def tile(w, h):
        return w[:, h * P:(h + 1) * P]

    parts = [wide_units(I)]
    for h in range(HEADS):
        parts += [tall_units(tile(FF, h)), tall_units(tile(FB, h))]
    parts += [wide_units(I[:, :512]), tall_units(I[:, 512:])]
    for h in range(HEADS):
        parts += [tall_units(tile(w, h)) for w in (Q, FF, FB, G)]
    parts += [tall_units(U), wide_units(V), wide_units(np.concatenate([w_out[1024:], w_out[:1024]], 0))]
    for b in range(BLOCKS):
        s = slice(1024 * b, 1024 * (b + 1))
        first = tall_units(w1[:, s])
        if b == 0:
            first[[1, 2]] = first[[2, 1]]
        parts += [first, wide_units(w2[s])]
    stream = np.concatenate(parts, 0)
    assert stream.shape[0] == UNITS

    def columns(v):
        return v.reshape(-1, P).T

    b_ada = a["b_ada"][0]
    cond = np.stack([columns(a["c"][0]), columns(a["c_ctx"])], 2).reshape(P, 2 * KT)
    cols = np.concatenate([cond, columns(b_ada), columns(a["norm1_gain"][0]), columns(a["norm2_gain"][0]),
                           a["gmlp_v_gain"][0].T, a["hgrn_o_gain"][0].T, np.zeros((P, 16), np.float32)], 1)
    small = a["hgrn_lb_logits"].reshape(2, 2, HEADS, P).transpose(3, 0, 1, 2).reshape(P, 4 * HEADS)
    t = np.arange(P)
    mask = np.stack([((t[:, None] >> i) == (t[None, :] >> i) ^ 1) for i in range(LEVELS)], 1).astype(np.float32)
    arrays = {
        "ctx_x": a["ctx"][0], "x": a["x"][0], "w_stream": stream, "w_ada": a["w_ada"][0], "cols": cols, "small": small,
        "ident": np.eye(P, dtype=np.float32), "mask": mask, "bs_row": a["gmlp_b_s"][0], "final_row": a["final_gain"],
        "ws_t": a["gmlp_w_s"][0].transpose(2, 0, 1),
    }
    arrays = {f"in_{k}": np.ascontiguousarray(v) for k, v in arrays.items()}
    nc = bacc.Bacc("TRN2", target_bir_lowering=False, num_devices=1)
    ap = {k[3:]: nc.dram_tensor(k, v.shape, mybir.dt.from_np(v.dtype), kind="ExternalInput").ap() for k, v in arrays.items()}
    out = nc.dram_tensor("out", (SEQ, D), F32, kind="ExternalOutput").ap()
    build(nc, ap["ctx_x"], ap["x"], ap["w_stream"], ap["w_ada"], ap["cols"], ap["small"], (ap["ident"], ap["mask"]),
          ap["bs_row"], ap["final_row"], ap["ws_t"], out)
    return run(nc, [arrays], core_ids=[0]).results[0]["out"].reshape(1, SEQ, D)
```
